# Optimizing a Trainium2 kernel written in Bass

```python
import jax
import jax.numpy as jnp
from jax import lax
import numpy as np

D_MODEL = 1024
BATCH = 1
SEQ = 256
DEPTH = 1

CHUNK = 64
D_MIX = D_MODEL
D_CONV = D_MIX // 2
D_LRU = D_MIX - D_CONV
CONV_GROUPS = 8
LRU_HEADS = 8
LRU_HEAD_DIM = D_LRU // LRU_HEADS
SHORT_CONV_WIDTH = 3
LRU_CONV_WIDTH = 4
LRU_C = 8.0
IN_COLS = 3 * D_CONV + 2 * D_LRU
N_EXPERTS = 32
TOP_K = 4
D_EXPERT = D_MODEL
SWIGLU_LIMIT = 7.0
SWIGLU_ALPHA = 1.702
EXPERT_BLOCK = 256
LN_EPS = 1e-5
DEEPNORM_ALPHA = (2.0 * DEPTH) ** 0.25
DEEPNORM_BETA = (8.0 * DEPTH) ** -0.25

kernel_name = "hybrid_conv_rglru_moe_deepnorm"

def _layer_norm(x, g, b):
    xf = x.astype(jnp.float32)
    mu = jnp.mean(xf, axis=-1, keepdims=True)
    var = jnp.mean(jnp.square(xf - mu), axis=-1, keepdims=True)
    return ((xf - mu) * lax.rsqrt(var + LN_EPS) * g.astype(jnp.float32) + b.astype(jnp.float32)).astype(x.dtype)

def _causal_depthwise_conv(u, w):
    k = w.shape[0]
    return lax.conv_general_dilated(
        u, w[:, None, :].astype(u.dtype), window_strides=(1,), padding=[(k - 1, 0)],
        dimension_numbers=('NWC', 'WIO', 'NWC'), feature_group_count=u.shape[-1])

def _linear_recurrence_combine(left, right):
    a_l, b_l = left
    a_r, b_r = right
    return a_l * a_r, a_r * b_l + b_r

def _rg_lru(u, w_r, b_r, w_i, b_i, lam):
    bsz, seq, width = u.shape
    uh = u.reshape(bsz, seq, LRU_HEADS, LRU_HEAD_DIM)
    r = jax.nn.sigmoid((jnp.einsum('bshi,hij->bshj', uh, w_r).reshape(bsz, seq, width) + b_r).astype(jnp.float32))
    i = jax.nn.sigmoid((jnp.einsum('bshi,hij->bshj', uh, w_i).reshape(bsz, seq, width) + b_i).astype(jnp.float32))
    log_a = -LRU_C * r * jax.nn.softplus(-lam.astype(jnp.float32))
    a = jnp.exp(log_a)
    b = jnp.sqrt(-jnp.expm1(2.0 * log_a)) * (i * u.astype(jnp.float32))
    _, h = lax.associative_scan(_linear_recurrence_combine, (a, b), axis=1)
    return h.astype(u.dtype)

def _mixer(x, w_in, conv_w, lru_conv_w, lru_conv_b, w_rgate, b_rgate, w_igate, b_igate, lru_lambda, w_out):
    proj = jnp.einsum('bsd,dc->bsc', x, w_in)
    c_b, c_c, c_h, r_x, r_g = jnp.split(
        proj, [D_CONV, 2 * D_CONV, 3 * D_CONV, 3 * D_CONV + D_LRU], axis=-1)
    y_conv = c_b * _causal_depthwise_conv(c_c * c_h, conv_w)
    u = _causal_depthwise_conv(r_x, lru_conv_w) + lru_conv_b
    y_lru = _rg_lru(u, w_rgate, b_rgate, w_igate, b_igate, lru_lambda) * jax.nn.gelu(r_g)
    mix = jnp.concatenate([y_conv, y_lru], axis=-1)
    return jnp.einsum('bsc,cd->bsd', mix, w_out)

def _moe(x, w_router, b_router, w_gu, b_gu, w_dn, b_dn):
    bsz, seq, d = x.shape
    n_tok = bsz * seq
    n_assign = n_tok * TOP_K
    n_blocks = -(-n_assign // EXPERT_BLOCK) + N_EXPERTS
    xt = x.reshape(n_tok, d)
    logits = (xt @ w_router + b_router).astype(jnp.float32)
    top_v, top_e = lax.top_k(logits, TOP_K)
    gates = jax.nn.softmax(top_v, axis=-1).astype(x.dtype)
    flat_e = top_e.reshape(-1)
    order = jnp.argsort(flat_e)
    e_sorted = flat_e[order]
    counts = jnp.bincount(flat_e, length=N_EXPERTS)
    padded = (counts + EXPERT_BLOCK - 1) // EXPERT_BLOCK * EXPERT_BLOCK
    pad_end = jnp.cumsum(padded)
    pad_start = pad_end - padded
    grp_start = jnp.cumsum(counts) - counts
    dest = pad_start[e_sorted] + jnp.arange(n_assign) - grp_start[e_sorted]
    x_pad = jnp.zeros((n_blocks * EXPERT_BLOCK, d), x.dtype).at[dest].set(xt[order // TOP_K])
    block_e = jnp.minimum(
        jnp.searchsorted(pad_end, jnp.arange(n_blocks) * EXPERT_BLOCK, side='right'), N_EXPERTS - 1)

    def expert_block(args):
        xb, e = args
        h = xb @ w_gu[e] + b_gu[e]
        h_glu = jnp.minimum(h[:, :D_EXPERT], SWIGLU_LIMIT)
        h_lin = jnp.clip(h[:, D_EXPERT:], -SWIGLU_LIMIT, SWIGLU_LIMIT)
        act = h_glu * jax.nn.sigmoid(SWIGLU_ALPHA * h_glu) * (h_lin + 1.0)
        return act @ w_dn[e] + b_dn[e]

    y_pad = lax.map(expert_block, (x_pad.reshape(n_blocks, EXPERT_BLOCK, d), block_e))
    y_pad = y_pad.reshape(n_blocks * EXPERT_BLOCK, d)
    slot = jnp.zeros((n_assign,), dest.dtype).at[order].set(dest)
    y = y_pad[slot].reshape(n_tok, TOP_K, d)
    return jnp.einsum('tkd,tk->td', y, gates).reshape(bsz, seq, d)

def setup_inputs(seed: int = 0) -> dict:
    key = jax.random.key(seed)
    ks = jax.random.split(key, 22)
    f32 = jnp.float32
    nrm = lambda k, shape, s: jax.random.normal(k, shape, f32) * s
    u = jax.random.uniform(ks[11], (DEPTH, D_LRU), f32, minval=0.9, maxval=0.999)
    s = u ** (1.0 / LRU_C)
    lru_lambda = jnp.log(s) - jnp.log1p(-s)
    return {
        "x": nrm(ks[0], (BATCH, SEQ, D_MODEL), 1.0),
        "w_in": nrm(ks[1], (DEPTH, D_MODEL, IN_COLS), D_MODEL ** -0.5),
        "conv_w": nrm(ks[2], (DEPTH, SHORT_CONV_WIDTH, D_CONV), SHORT_CONV_WIDTH ** -0.5),
        "lru_conv_w": nrm(ks[3], (DEPTH, LRU_CONV_WIDTH, D_LRU), LRU_CONV_WIDTH ** -0.5),
        "lru_conv_b": nrm(ks[4], (DEPTH, D_LRU), 0.01),
        "w_rgate": nrm(ks[5], (DEPTH, LRU_HEADS, LRU_HEAD_DIM, LRU_HEAD_DIM), LRU_HEAD_DIM ** -0.5),
        "b_rgate": nrm(ks[6], (DEPTH, D_LRU), 0.01),
        "w_igate": nrm(ks[7], (DEPTH, LRU_HEADS, LRU_HEAD_DIM, LRU_HEAD_DIM), LRU_HEAD_DIM ** -0.5),
        "b_igate": nrm(ks[8], (DEPTH, D_LRU), 0.01),
        "lru_lambda": lru_lambda,
        "w_out": nrm(ks[9], (DEPTH, D_MIX, D_MODEL), D_MIX ** -0.5 * DEEPNORM_BETA),
        "ln1_g": 1.0 + nrm(ks[10], (DEPTH, D_MODEL), 0.02),
        "ln1_b": nrm(ks[12], (DEPTH, D_MODEL), 0.02),
        "w_router": nrm(ks[13], (DEPTH, D_MODEL, N_EXPERTS), D_MODEL ** -0.5),
        "b_router": nrm(ks[14], (DEPTH, N_EXPERTS), 0.01),
        "w_gate_up": nrm(ks[15], (DEPTH, N_EXPERTS, D_MODEL, 2 * D_EXPERT), D_MODEL ** -0.5),
        "b_gate_up": nrm(ks[16], (DEPTH, N_EXPERTS, 2 * D_EXPERT), 0.01),
        "w_down": nrm(ks[17], (DEPTH, N_EXPERTS, D_EXPERT, D_MODEL), D_EXPERT ** -0.5 * DEEPNORM_BETA),
        "b_down": nrm(ks[18], (DEPTH, N_EXPERTS, D_MODEL), 0.01),
        "ln2_g": 1.0 + nrm(ks[19], (DEPTH, D_MODEL), 0.02),
        "ln2_b": nrm(ks[20], (DEPTH, D_MODEL), 0.02),
    }

def reference(x, w_in, conv_w, lru_conv_w, lru_conv_b, w_rgate, b_rgate, w_igate, b_igate, lru_lambda,
              w_out, ln1_g, ln1_b, w_router, b_router, w_gate_up, b_gate_up, w_down, b_down, ln2_g, ln2_b):
    for l in range(DEPTH):
        mixed = _mixer(x, w_in[l], conv_w[l], lru_conv_w[l], lru_conv_b[l], w_rgate[l], b_rgate[l],
                       w_igate[l], b_igate[l], lru_lambda[l], w_out[l])
        x = _layer_norm(DEEPNORM_ALPHA * x + mixed, ln1_g[l], ln1_b[l])
        ffn = _moe(x, w_router[l], b_router[l], w_gate_up[l], b_gate_up[l], w_down[l], b_down[l])
        x = _layer_norm(DEEPNORM_ALPHA * x + ffn, ln2_g[l], ln2_b[l])
    return x


_drawn_inputs = setup_inputs


def setup_inputs(seed=0):
    import zlib

    import numpy as np

    out = dict(_drawn_inputs(seed))
    spreads = {}
    factors = {'lru_conv_b': 3.111,
     'b_rgate': 64.0,
     'b_igate': 44.491,
     'b_router': 3.451,
     'b_gate_up': 8.0,
     'b_down': 8.0,
     'ln2_g': 8.054,
     'ln2_b': 8.37}
    for name, (base, spread) in spreads.items():
        noise = np.random.default_rng([zlib.crc32(name.encode()), seed]).standard_normal(out[name].shape)
        drawn = base * np.exp(spread * noise) if base else spread * noise
        out[name] = jnp.asarray(drawn.astype(out[name].dtype))
    for name, factor in factors.items():
        out[name] = (out[name] * factor).astype(out[name].dtype)
    return out
```

```python
from contextlib import ExitStack

import concourse.bass as bass
from concourse import mybir

F32 = mybir.dt.float32
BF16 = mybir.dt.bfloat16
I32 = mybir.dt.int32
U32 = mybir.dt.uint32
ALU = mybir.AluOpType
ACT = mybir.ActivationFunctionType
AX = mybir.AxisListType

P = 128
SLOTS = 32
GROUPS = P // SLOTS
LRU_C = 8.0
SWIGLU_LIMIT = 7.0
SWIGLU_ALPHA = 1.702
LN_EPS = 1e-5
TOP_K = 4
GELU_IN = 2.0 * (2.0 / 3.141592653589793) ** 0.5
GELU_CUBE = 0.044715
TINY = 1e-35


def trunk(nc, x, w_in, conv_w, lru_conv_w, lru_conv_b, w_rgate, b_rgate, w_igate, b_igate, lru_lambda, w_out,
          ln1_g, ln1_b, w_router, b_router, w_gate_up, b_gate_up, w_down, b_down, ln2_g, ln2_b, out):
    SEQ, D = x.shape[1], x.shape[2]
    KT = D // P
    TH = SEQ // P
    C = D // 2
    CT = C // P
    E = w_router.shape[2]
    F = w_down.shape[2]
    HD = w_rgate.shape[2]
    CW = conv_w.shape[1]
    LW = lru_conv_w.shape[1]
    alpha = (2.0 * x.shape[0]) ** 0.25
    assert (SEQ, D, E, F) == (256, 1024, 32, 1024) and 2 * HD == P
    QF = F // GROUPS
    MAXB = TOP_K * SEQ // SLOTS + E
    GC = 4
    DC = 2
    GK = KT // GC
    PIECE = 512
    RX, RG, CC, CH, CB = range(5)
    COLS = {RX: 3 * C, RG: 3 * C + C, CC: C, CH: 2 * C, CB: 0}

    with ExitStack() as ctx:
        def sb(name, shape, dt=F32):
            return ctx.enter_context(nc.sbuf_tensor(name, shape, dt))

        def sem(name):
            return ctx.enter_context(nc.semaphore(name))

        gu_buf = sb("gu_buf", [P, 2, KT, 2 * F])
        dn_buf = sb("dn_buf", [P, DC, GROUPS, D])
        xs = sb("xs", [P, TH, D])
        turned = sb("turned", [P, KT, SEQ])
        mix = sb("mix", [P, KT, SEQ])
        late = sb("late", [P, 2, D])
        wr = sb("wr", [P, KT, E])
        ident = sb("ident", [P, P])
        stack_ident = sb("stack_ident", [P, E])
        slot_iota = sb("slot_iota", [P, GROUPS, SLOTS])
        before = sb("before", [P, P], BF16)
        ones_bf = sb("ones_bf", [P, P], BF16)
        block_base = sb("block_base", [P, MAXB + 1])
        part_iota = sb("part_iota", [P, 1])
        b_rout = sb("b_rout", [P, E])
        onehot = sb("onehot", [P, TH, GROUPS, SLOTS])
        gated = sb("gated", [P, TH, P])
        back = sb("back", [P, TH * P])
        rows = sb("rows", [P, QF])
        rows_t = sb("rows_t", [P, 2, P])
        glu = sb("glu", [P, QF])
        lin = sb("lin", [P, QF])
        sig = sb("sig", [P, QF])
        act_t = sb("act_t", [P, 2, P])
        bias_sel = sb("bias_sel", [P, SLOTS])
        places = sb("places", [P, TH, E])
        gates = sb("gates", [P, TH, E])
        small = sb("small", [P, 384])
        bounds = sb("bounds", [1, E + 1], I32)
        expert_of = sb("expert_of", [1, P], I32)

        w_piece = gu_buf[:, 1].rearrange("p (s a) (b n) -> p s (a b) n", s=4, n=PIECE)
        piece_slot = {RX: 0, RG: 1, CC: 2, CH: 3, CB: 0}
        w_out_v = gu_buf[:, 1, 2:6].rearrange("p a (b n) -> p (a b) n", n=D)
        ln1_v = gu_buf[:, 1, 6:7].rearrange("p a (b n) -> p (a b) n", n=D)
        b_dn_v = gu_buf[:, 1, 0:1, 0:D].rearrange("p a n -> p (a n)")
        pad_v = gu_buf[:, 1, 1:2, 0:2 * P].rearrange("p a (b n) -> p (a b) n", n=P)
        gatesT_v = gu_buf[:, 1, 1:2, 2 * P:4 * P].rearrange("p a n -> p (a n)")
        scratch = dn_buf[:].rearrange("p m j n -> p (m j n)")
        at = [0]

        def take(n):
            at[0] += n
            return scratch[:, at[0] - n:at[0]]
        rx = take(CT * (SEQ + LW - 1)).rearrange("p (i t) -> p i t", i=CT)
        cv = take(CT * (SEQ + CW - 1)).rearrange("p (i t) -> p i t", i=CT)
        u, rgate, igate, rec, gel = [take(CT * SEQ).rearrange("p (i t) -> p i t", i=CT) for _ in range(5)]
        params_in = take(P)
        gel2 = rx[:, :, 0:SEQ]
        wr_bd = late[:, 0, 0:CT * P].rearrange("p (i n) -> p i n", i=CT)
        wi_bd = late[:, 1, 0:CT * P].rearrange("p (i n) -> p i n", i=CT)
        y_sb = mix[:].rearrange("p k t -> p (k t)")[:, 0:D]
        x1t = mix
        b_gu = turned[:].rearrange("p k t -> p (k t)")
        prm = small[:, 0:64]
        N_PRM = CT * (LW + CW + 4)
        off_lw, off_cw, off_lb, off_br, off_bi, off_lam = [CT * v for v in (0, LW, LW + CW, LW + CW + 1, LW + CW + 2, LW + CW + 3)]

        ps = ctx.enter_context(nc.psum_tensor("ps", [P, 8, 512], F32))
        HB, Y0, Y1, TB = 4, 5, 6, 7

        def half(bank, n):
            return ps[:, bank, 256 * n:256 * n + 256]

        S = {n: sem(n) for n in (
            "consts", "x_in", "params_zero", "params_loaded", "bd_zero", "bd_in", "small_in", "wout_in", "ln1_in", "bdn_zero", "bdn_in",
            "bgu_zero", "bgu_in", "ln2_in",
            "params_t", "params_ok", "xt_ps", "xt_sb_act", "xt_sb_dve", "proj", "rx_sb", "rg_sb", "cc_sb", "u_ok",
            "sp_ok", "gates_ps", "gate_sb", "tanh_ok", "sqrt_ok", "gelu_in", "gelu_sig", "cb_used", "ch_used",
            "mix_lru", "mix_conv", "out_ps", "ln1_in_ok", "var_ok", "rstd_ok", "x1_ok", "x1t_ps", "x1t_act", "x1t_dve", "lpart_ps",
            "lpart_sb", "logits_ps", "exp_in", "exp_ok", "gates_ok", "gpad_ps", "gpad_sb", "sel_ok", "pos_ps", "cnt_ok", "cnt_ps",
            "bounds_ok", "acc_started", "onehot0", "rows0_ps", "rows0_sb", "rows0t_ps",
            "dve_link", "pool_link", "lam_ok", "lam_sig", "tanh_kept", "scaled",
            "rows_t_ok", "sel_bias", "h_ps", "onehot_ok", "y0_sb", "y1_sb", "back_sb", "rows_ps", "gated_ok",
            "back_ps", "act_ok", "act_t_ps", "rows_sb", "rows_t_ps", "act_t_sb", "y_ps", "glu_ok", "lin_ok", "sig_ok",
            "acc_done", "fin_var", "fin_rstd", "fin_ok", "stored")}
        w_in_s = [sem(f"w_in{i}") for i in range(5)]
        gu_in = [[sem(f"gu_in{b}{c}") for c in range(GC)] for b in range(2)]
        dn_in = [sem(f"dn_in{c}") for c in range(DC)]
        gu_used = [sem(f"gu_used{c}") for c in range(GC - 1)] + [S["h_ps"]]
        dn_used = [sem("dn_used0"), S["y_ps"]]

        gu_src = w_gate_up[0].rearrange("e (k p) n -> e p k n", p=P)
        dn_src = w_down[0].rearrange("e (j m p) n -> e m p j n", p=P, m=DC)
        w_in_src = w_in[0].rearrange("(k p) n -> p k n", p=P)
        x_src = x[0].rearrange("(h p) d -> p h d", p=P)
        out_dst = out[0].rearrange("(h p) d -> p h d", p=P)

        block = ctx.enter_context(nc.Block())

        @block.sync
        def _(sp):
            def load_gu(e, b, c):
                return sp.dma_start(gu_buf[:, b, GK * c:GK * (c + 1), :], gu_src[e][:, GK * c:GK * (c + 1), :]).then_inc(gu_in[b][c], 16)

            def load_dn(e, c):
                return sp.dma_start(dn_buf[:, c], dn_src[e, c]).then_inc(dn_in[c], 16)

            sp.dma_start(xs[:], x_src).then_inc(S["x_in"], 16)
            for i in (RX, RG, CC, CH, CB):
                if i == CB:
                    sp.wait_ge(S["proj"], 1)
                sp.dma_start(w_piece[:, piece_slot[i]], w_in_src[:, :, COLS[i]:COLS[i] + PIECE]).then_inc(w_in_s[i], 16)
            for c in range(GC):
                load_gu(0, 0, c)
            sp.wait_ge(S["proj"], 3)
            sp.dma_start(w_out_v, w_out[0].rearrange("(k p) n -> p k n", p=P)).then_inc(S["wout_in"], 16)
            sp.wait_ge(S["proj"], 4)
            sp.dma_start(ln1_v[:, 0, :], ln1_g[0:1, :].to_broadcast([P, D])).then_inc(S["ln1_in"], 16)
            sp.dma_start(ln1_v[:, 1, :], ln1_b[0:1, :].to_broadcast([P, D])).then_inc(S["ln1_in"], 16)
            sp.wait_ge(S["proj"], 5)
            sp.wait_ge(S["bgu_zero"], 1)
            sp.dma_start(b_gu[0:E, :], b_gate_up[0]).then_inc(S["bgu_in"], 16)
            sp.wait_ge(S["bdn_zero"], 1)
            sp.dma_start(b_dn_v[0:E, :], b_down[0]).then_inc(S["bdn_in"], 16)
            sp.wait_ge(S["out_ps"], 1)
            for c in range(DC):
                load_dn(0, c)
            sp.wait_ge(S["gates_ps"], 2)
            sp.dma_start(late[:, 0, :], ln2_g[0:1, :].to_broadcast([P, D])).then_inc(S["ln2_in"], 16)
            sp.dma_start(late[:, 1, :], ln2_b[0:1, :].to_broadcast([P, D])).then_inc(S["ln2_in"], 16)
            for c in (1, 2):
                load_gu(1, 1, c)
            sp.wait_ge(S["x1_ok"], 2)
            load_gu(1, 1, 3)
            sp.wait_ge(S["acc_started"], 1)
            load_gu(1, 1, 0)
            sp.wait_ge(S["bounds_ok"], 1)
            done = sp.value_load(bounds[0:1, 1:2], min_val=1, max_val=MAXB)
            for c in range(DC):
                sp.wait_ge(dn_used[c], done)
                load_dn(1, c)
            with sp.Fori(1, E // 2) as pair:
                for b in range(2):
                    e = pair * 2 + b
                    before_last = sp.value_load(bounds[0:1, bass.ds(pair * 2 + (b - 1), 1)], min_val=1, max_val=MAXB)
                    for c in range(GC):
                        sp.wait_ge(gu_used[c], before_last)
                        sp.dma_start(gu_buf[:, b, GK * c:GK * (c + 1), :],
                                     gu_src[bass.ds(e, 1)].rearrange("o p k n -> p (o k) n")[:, GK * c:GK * (c + 1), :]).then_inc(gu_in[b][c], 16)
                    last = sp.value_load(bounds[0:1, bass.ds(e, 1)], min_val=1, max_val=MAXB)
                    for c in range(DC):
                        sp.wait_ge(dn_used[c], last)
                        sp.dma_start(dn_buf[:, c], dn_src[bass.ds(e, 1), c].rearrange("o p j n -> p (o j) n")).then_inc(dn_in[c], 16)
            for h in range(TH):
                sp.wait_ge(S["fin_ok"], h + 1)
                sp.dma_start(out_dst[:, h, :], xs[:, h, :]).then_inc(S["stored"], 16)
            sp.wait_ge(S["stored"], 16 * TH)

        @block.gpsimd
        def _(pool):
            links = [0]

            def link(ins):
                links[0] += 1
                ins.then_inc(S["pool_link"], 1)
                pool.wait_ge(S["pool_link"], links[0])

            nc.gpsimd.memset(params_in, 0.0).then_inc(S["params_zero"], 1)
            link(nc.gpsimd.memset(ident[:], 0.0))
            link(nc.gpsimd.affine_select(out=ident[:], in_=ident[:], compare_op=ALU.not_equal, fill=1.0, base=0,
                                         pattern=[[-1, P]], channel_multiplier=1))
            nc.gpsimd.memset(late[:, 0, 0:CT * P], 0.0).then_inc(S["bd_zero"], 1)
            nc.gpsimd.memset(late[:, 1, 0:CT * P], 0.0).then_inc(S["bd_zero"], 1)
            nc.gpsimd.iota(slot_iota[:], pattern=[[0, GROUPS], [1, SLOTS]], base=0, channel_multiplier=0,
                           allow_small_or_imprecise_dtypes=True)
            nc.gpsimd.iota(block_base[:], pattern=[[SLOTS, MAXB + 1]], base=0, channel_multiplier=0,
                           allow_small_or_imprecise_dtypes=True)
            nc.gpsimd.iota(part_iota[:], pattern=[[0, 1]], base=0, channel_multiplier=1,
                           allow_small_or_imprecise_dtypes=True)
            link(nc.gpsimd.memset(gated[:, 0, :], 1.0))
            link(nc.gpsimd.affine_select(out=gated[:, 1, :], in_=gated[:, 0, :], compare_op=ALU.is_gt, fill=0.0, base=0,
                                         pattern=[[1, P]], channel_multiplier=-1))
            link(nc.gpsimd.tensor_copy(before[:], gated[:, 1, :]))
            link(nc.gpsimd.tensor_copy(ones_bf[:], gated[:, 0, :]))
            nc.gpsimd.memset(small[:, 380:382], -0.5).then_inc(S["consts"], 1)
            pool.wait_ge(S["proj"], 5)
            nc.gpsimd.memset(b_gu, 0.0).then_inc(S["bgu_zero"], 1)
            link(nc.gpsimd.memset(pad_v, 0.0))
            nc.gpsimd.memset(b_dn_v, 0.0).then_inc(S["bdn_zero"], 1)
            for h in range(TH):
                pool.wait_ge(S["var_ok"], h + 1)
                nc.gpsimd.tensor_tensor(small[:, 374 + h:375 + h], small[:, 370 + h:371 + h], small[:, 380:381], ALU.pow).then_inc(S["rstd_ok"], 1)
            for h in range(TH):
                pool.wait_ge(S["fin_var"], h + 1)
                nc.gpsimd.tensor_tensor(small[:, 374 + h:375 + h], small[:, 370 + h:371 + h], small[:, 380:381], ALU.pow).then_inc(S["fin_rstd"], 1)

        @block.scalar
        def _(act):
            act.wait_ge(S["params_zero"], 1)
            row = 0
            for src, n in ((lru_conv_w[0].rearrange("k (i p) -> (k i) p", p=P), LW), (conv_w[0].rearrange("k (i p) -> (k i) p", p=P), CW),
                           (lru_conv_b[0].rearrange("(i p) -> i p", p=P), 1), (b_rgate[0].rearrange("(i p) -> i p", p=P), 1),
                           (b_igate[0].rearrange("(i p) -> i p", p=P), 1), (lru_lambda[0].rearrange("(i p) -> i p", p=P), 1)):
                act.dma_start(params_in[row:row + n * CT, :], src).then_inc(S["params_loaded"], 16)
                row += n * CT
            act.wait_ge(S["bd_zero"], 2)
            for dst, src in ((wr_bd, w_rgate), (wi_bd, w_igate)):
                heads = src[0].rearrange("(i two) r c -> two r i c", two=2)
                for s in range(2):
                    act.dma_start(dst[HD * s:HD * (s + 1), :, HD * s:HD * (s + 1)], heads[s]).then_inc(S["bd_in"], 16)
            act.dma_start(wr[:], w_router[0].rearrange("(k p) e -> p k e", p=P)).then_inc(S["small_in"], 16)
            act.dma_start(b_rout[:], b_router[0:1, :].to_broadcast([P, E])).then_inc(S["small_in"], 16)

            for b in (0, 2):
                act.wait_ge(S["xt_ps"], b + 1)
                nc.scalar.copy(turned[:, 2 * b:2 * b + 2, :], ps[:, b, :].rearrange("p (k t) -> p k t", k=2)).then_inc(S["xt_sb_act"], 1)
            act.wait_ge(S["lam_ok"], 1)
            nc.scalar.activation(small[:, 80:84], small[:, 76:80], ACT.Sigmoid).then_inc(S["lam_sig"], 1)
            act.wait_ge(S["proj"], 1)
            for b in range(2):
                nc.scalar.copy(rx[:, 2 * b:2 * b + 2, LW - 1:], ps[:, 4 + b, :].rearrange("p (i t) -> p i t", i=2)).then_inc(S["rx_sb"], 1)
            act.wait_ge(S["proj"], 2)
            for b in range(2):
                nc.scalar.copy(gel[:, 2 * b:2 * b + 2, :], ps[:, 6 + b, :].rearrange("p (i t) -> p i t", i=2)).then_inc(S["rg_sb"], 1)
            for n, (dst, off) in enumerate(((rgate, off_br), (igate, off_bi))):
                act.wait_ge(S["gates_ps"], n + 1)
                act.wait_ge(S["params_ok"], 1)
                for i in range(CT):
                    nc.scalar.activation(dst[:, i, :], half(4 + 2 * n + i // 2, i % 2), ACT.Sigmoid,
                                         bias=prm[:, off + i:off + i + 1]).then_inc(S["gate_sb"], 1)
            act.wait_ge(S["sp_ok"], 1)
            act.wait_ge(S["gate_sb"], CT)
            for i in range(CT):
                nc.scalar.activation(rgate[:, i, :], rgate[:, i, :], ACT.Tanh, scale=small[:, 64 + i:65 + i]).then_inc(S["tanh_ok"], 1)
            act.wait_ge(S["gelu_in"], 1)
            nc.scalar.activation(gel2, gel2, ACT.Sigmoid, scale=GELU_IN).then_inc(S["gelu_sig"], 1)
            act.wait_ge(S["tanh_kept"], 1)
            nc.scalar.activation(rgate, rgate, ACT.Sqrt).then_inc(S["sqrt_ok"], 1)
            act.wait_ge(S["proj"], 3)
            for b in range(2):
                nc.scalar.copy(cv[:, 2 * b:2 * b + 2, CW - 1:], ps[:, b, :].rearrange("p (i t) -> p i t", i=2)).then_inc(S["cc_sb"], 1)
            for b in (0, 2):
                act.wait_ge(S["x1t_ps"], b + 1)
                nc.scalar.copy(x1t[:, 2 * b:2 * b + 2, :], ps[:, 4 + b, :].rearrange("p (k t) -> p k t", k=2)).then_inc(S["x1t_act"], 1)
            act.wait_ge(S["lpart_ps"], 1)
            nc.scalar.copy(glu[:], half(HB, 0)).then_inc(S["lpart_sb"], 1)
            act.wait_ge(S["exp_in"], 1)
            nc.scalar.activation(small[:, 128:192], small[:, 64:128], ACT.Sigmoid).then_inc(S["exp_ok"], 1)
            act.wait_ge(S["gpad_ps"], 1)
            nc.scalar.copy(gatesT_v[0:E, :], ps[0:E, Y1, 0:SEQ]).then_inc(S["gpad_sb"], 1)
            act.wait_ge(S["rows0_ps"], 1)
            nc.scalar.copy(rows[:], half(Y0, 0)).then_inc(S["rows0_sb"], 1)
            act.wait_ge(S["rows0t_ps"], 1)
            nc.scalar.copy(rows_t[:], half(HB, 0).rearrange("p (b s) -> p b s", b=2)).then_inc(S["rows_t_ok"], 1)

            act.wait_ge(S["bounds_ok"], 1)
            n_blocks = act.value_load(bounds[0:1, E:E + 1], min_val=1, max_val=MAXB)
            with act.Fori(0, n_blocks) as g:
                now = g + 1
                act.wait_ge(S["glu_ok"], now)
                nc.scalar.activation(sig[:], glu[:], ACT.Sigmoid, scale=SWIGLU_ALPHA).then_inc(S["sig_ok"], 1)
                act.wait_ge(S["rows_ps"], now)
                nc.scalar.copy(rows[:], half(Y0, 0)).then_inc(S["rows_sb"], 1)
                act.wait_ge(S["back_ps"], now)
                nc.scalar.copy(back[:], half(Y1, 0)).then_inc(S["back_sb"], 1)
                act.wait_ge(S["rows_t_ps"], now)
                nc.scalar.copy(rows_t[:], half(HB, 0).rearrange("p (b s) -> p b s", b=2)).then_inc(S["rows_t_ok"], 1)
                act.wait_ge(S["y_ps"], now)
                nc.scalar.copy(y_sb[:, 0:512], ps[:, Y0, :]).then_inc(S["y0_sb"], 1)

        @block.vector
        def _(dve):
            V = nc.vector
            links = [0]

            def link(ins):
                links[0] += 1
                ins.then_inc(S["dve_link"], 1)
                dve.wait_ge(S["dve_link"], links[0])

            V.memset(rx[:, :, 0:LW - 1], 0.0)
            V.memset(cv[:, :, 0:CW - 1], 0.0)
            dve.wait_ge(S["params_t"], 1)
            V.tensor_copy(prm, ps[:, HB, 0:64]).then_inc(S["params_ok"], 1)
            for b in (1, 3):
                dve.wait_ge(S["xt_ps"], b + 1)
                V.tensor_copy(turned[:, 2 * b:2 * b + 2, :], ps[:, b, :].rearrange("p (k t) -> p k t", k=2)).then_inc(S["xt_sb_dve"], 1)
            lam = prm[:, off_lam:off_lam + CT]
            t = [small[:, 72 + CT * i:72 + CT * (i + 1)] for i in range(6)]
            dve.wait_ge(S["params_ok"], 1)
            link(V.tensor_scalar(t[0], lam, -1.0, None, ALU.mult))
            link(V.tensor_tensor(t[1], t[0], lam, ALU.min))
            V.tensor_scalar(t[5], t[0], 0.0, None, ALU.max).then_inc(S["lam_ok"], 1)
            dve.wait_ge(S["lam_sig"], 1)
            link(V.tensor_scalar(t[3], t[2], -1.0, 2.0, ALU.mult, ALU.add))
            link(V.reciprocal(t[4], t[3]))
            link(V.tensor_tensor(t[0], t[2], t[4], ALU.mult))
            link(V.tensor_tensor(t[1], t[0], t[0], ALU.mult))
            link(V.memset(t[3], 1.0 / 17))
            for n in range(7, -1, -1):
                link(V.tensor_tensor(t[4], t[3], t[1], ALU.mult))
                link(V.tensor_scalar(t[3], t[4], 1.0 / (2 * n + 1), None, ALU.add))
            link(V.scalar_tensor_tensor(t[2], t[0], 2.0, t[3], ALU.mult, ALU.mult))
            link(V.tensor_tensor(t[4], t[2], t[5], ALU.add))
            V.tensor_scalar(small[:, 64:64 + CT], t[4], LRU_C / 2, None, ALU.mult).then_inc(S["sp_ok"], 1)
            for b in range(2):
                dve.wait_ge(S["rx_sb"], b + 1)
                for k in range(LW - 1, -1, -1):
                    for i in (2 * b, 2 * b + 1):
                        w = prm[:, off_lw + CT * k + i:off_lw + CT * k + i + 1]
                        if k == LW - 1:
                            ins = V.tensor_scalar(u[:, i, :], rx[:, i, k:k + SEQ], w, prm[:, off_lb + i:off_lb + i + 1], ALU.mult, ALU.add)
                        else:
                            ins = V.scalar_tensor_tensor(u[:, i, :], rx[:, i, k:k + SEQ], w, u[:, i, :], ALU.mult, ALU.add)
                    if k:
                        link(ins)
                ins.then_inc(S["u_ok"], 1)
            dve.wait_ge(S["rg_sb"], 2)
            dve.wait_ge(S["u_ok"], 2)
            link(V.tensor_tensor(gel2, gel, gel, ALU.mult))
            link(V.tensor_scalar(gel2, gel2, GELU_CUBE, 1.0, ALU.mult, ALU.add))
            V.tensor_tensor(gel2, gel2, gel, ALU.mult).then_inc(S["gelu_in"], 1)
            dve.wait_ge(S["tanh_ok"], CT)
            link(V.tensor_scalar(rec, rgate, 1.0, None, ALU.add))
            V.tensor_scalar(rgate, rgate, TINY, None, ALU.max).then_inc(S["tanh_kept"], 1)
            link(V.reciprocal(rec, rec))
            dve.wait_ge(S["gate_sb"], 2 * CT)
            link(V.tensor_tensor(igate, igate, u, ALU.mult))
            dve.wait_ge(S["sqrt_ok"], 1)
            link(V.scalar_tensor_tensor(rgate, rgate, 2.0, rec, ALU.mult, ALU.mult))
            link(V.tensor_tensor(igate, igate, rgate, ALU.mult))
            link(V.tensor_scalar(rec, rec, 2.0, -1.0, ALU.mult, ALU.add))
            for i in range(CT):
                ins = V.tensor_tensor_scan(u[:, i, :], rec[:, i, :], igate[:, i, :], 0.0, ALU.mult, ALU.add)
            link(ins)
            dve.wait_ge(S["gelu_sig"], 1)
            link(V.tensor_tensor(gel, gel, gel2, ALU.mult))
            V.tensor_tensor(mix[:, CT:KT, :], u, gel, ALU.mult).then_inc(S["mix_lru"], 1)
            dve.wait_ge(S["proj"], 4)
            dve.wait_ge(S["cc_sb"], 2)
            for b in range(2):
                V.tensor_tensor(cv[:, 2 * b:2 * b + 2, CW - 1:], cv[:, 2 * b:2 * b + 2, CW - 1:],
                                ps[:, 2 + b, :].rearrange("p (i t) -> p i t", i=2), ALU.mult).then_inc(S["ch_used"], 1)
            dve.wait_ge(S["ch_used"], 2)
            for k in range(CW):
                for i in range(CT):
                    w = prm[:, off_cw + CT * k + i:off_cw + CT * k + i + 1]
                    if k == 0:
                        ins = V.tensor_scalar(mix[:, i, :], cv[:, i, k:k + SEQ], w, None, ALU.mult)
                    else:
                        ins = V.scalar_tensor_tensor(mix[:, i, :], cv[:, i, k:k + SEQ], w, mix[:, i, :], ALU.mult, ALU.add)
                link(ins)
            dve.wait_ge(S["proj"], 5)
            for b in range(2):
                V.tensor_tensor(mix[:, 2 * b:2 * b + 2, :], mix[:, 2 * b:2 * b + 2, :],
                                ps[:, 4 + b, :].rearrange("p (i t) -> p i t", i=2), ALU.mult).then_inc(S["mix_conv"], 1)

            stats = small[:, 336:360].rearrange("p (h c s) -> p h c s", h=TH, c=2)
            mv = small[:, 360:364].rearrange("p (h s) -> p h s", h=TH)

            def layer_norm(g_ap, b_ap, var_sem, rstd_sem, ok_sem):
                for h in range(TH):
                    for c in range(2):
                        v = ps[:, 2 * h + c, :]
                        link(V.scalar_tensor_tensor(v, xs[:, h, 512 * c:512 * c + 512], alpha, v, ALU.mult, ALU.add))
                        link(V.bn_stats(stats[:, h, c, :], v))
                    link(V.bn_aggr(mv[:, h, :], stats[:, h, :, :]))
                    V.tensor_scalar(small[:, 370 + h:371 + h], mv[:, h, 1:2], LN_EPS, None, ALU.add).then_inc(var_sem, 1)
                    for c in range(2):
                        v = ps[:, 2 * h + c, :]
                        ins = V.scalar_tensor_tensor(v, v, mv[:, h, 0:1], g_ap[:, 512 * c:512 * c + 512], ALU.subtract, ALU.mult)
                    link(ins)
                for h in range(TH):
                    dve.wait_ge(rstd_sem, h + 1)
                    for c in range(2):
                        ins = V.scalar_tensor_tensor(xs[:, h, 512 * c:512 * c + 512], ps[:, 2 * h + c, :], small[:, 374 + h:375 + h],
                                                     b_ap[:, 512 * c:512 * c + 512], ALU.mult, ALU.add)
                    ins.then_inc(ok_sem, 1)

            dve.wait_ge(S["out_ps"], 1)
            dve.wait_ge(S["ln1_in"], 32)
            layer_norm(ln1_v[:, 0, :], ln1_v[:, 1, :], S["var_ok"], S["rstd_ok"], S["x1_ok"])
            for b in (1, 3):
                dve.wait_ge(S["x1t_ps"], b + 1)
                V.tensor_copy(x1t[:, 2 * b:2 * b + 2, :], ps[:, 4 + b, :].rearrange("p (k t) -> p k t", k=2)).then_inc(S["x1t_dve"], 1)
            dve.wait_ge(S["consts"], 1)
            V.tensor_reduce(stack_ident[:], ident[:].rearrange("p (j e) -> p e j", e=E), AX.X, ALU.add).then_inc(S["x1t_dve"], 1)
            lg = small[:, 0:64].rearrange("p (h e) -> p h e", h=TH)
            shifted = small[:, 64:128].rearrange("p (h e) -> p h e", h=TH)
            sg = small[:, 128:192].rearrange("p (h e) -> p h e", h=TH)
            sel = small[:, 192:256].rearrange("p (h e) -> p h e", h=TH)
            ex = small[:, 256:320].rearrange("p (h e) -> p h e", h=TH)
            top = small[:, 320:336].rearrange("p (h k) -> p h k", h=TH)
            idx = small[:, 336:352].bitcast(U32).rearrange("p (h k) -> p h k", h=TH)
            idxf = small[:, 352:368].rearrange("p (h k) -> p h k", h=TH)
            total = small[:, 368:370]
            eye_row = slot_iota[:, 0, :]
            dve.wait_ge(S["logits_ps"], 1)
            dve.wait_ge(S["small_in"], 32)
            dve.wait_ge(S["x1_ok"], 2)
            for h in range(TH):
                ins = V.tensor_tensor(lg[:, h, :], ps[:, Y0, E * h:E * (h + 1)], b_rout[:], ALU.add)
            link(ins)
            for h in range(TH):
                ins = V.max(top[:, h, :], lg[:, h, :])
            link(ins)
            for h in range(TH):
                ins = V.tensor_scalar(shifted[:, h, :], lg[:, h, :], top[:, h, 0:1], None, ALU.subtract)
            ins.then_inc(S["exp_in"], 1)
            for h in range(TH):
                ins = V.max_index(idx[:, h, :], top[:, h, :], lg[:, h, :])
            link(ins)
            link(V.tensor_copy(idxf, idx))
            for h in range(TH):
                ins = V.tensor_scalar(sel[:, h, :], eye_row, idxf[:, h, 0:1], None, ALU.is_equal)
            link(ins)
            for k in range(1, TOP_K):
                for h in range(TH):
                    ins = V.scalar_tensor_tensor(sel[:, h, :], eye_row, idxf[:, h, k:k + 1], sel[:, h, :], ALU.is_equal, ALU.add)
                link(ins)
            sel_bf = bias_sel[:].bitcast(BF16).rearrange("p (h e) -> p h e", h=TH)
            V.tensor_copy(sel_bf, sel).then_inc(S["sel_ok"], 1)
            dve.wait_ge(S["exp_ok"], 1)
            link(V.tensor_scalar(ex, sg, -1.0, 1.0, ALU.mult, ALU.add))
            link(V.reciprocal(ex, ex))
            link(V.tensor_tensor(ex, ex, sg, ALU.mult))
            link(V.tensor_tensor(ex, ex, sel, ALU.mult))
            link(V.tensor_reduce(total, ex, AX.X, ALU.add))
            link(V.reciprocal(total, total))
            for h in range(TH):
                V.tensor_scalar(gates[:, h, :], ex[:, h, :], total[:, h:h + 1], None, ALU.mult).then_inc(S["gates_ok"], 1)
            nb_i = small[:, 64:96].bitcast(I32)
            nb_s = small[:, 96:128].bitcast(I32)
            nb, ends, zero = small[:, 128:160], small[:, 160:192], small[:, 256:288]
            dve.wait_ge(S["pos_ps"], 1)
            dve.wait_ge(S["gates_ok"], TH)
            cnt = ps[:, TB, 2 * E:3 * E]
            link(V.tensor_scalar(nb_i, cnt, 1.0, SLOTS - 1.0, ALU.max, ALU.add))
            link(V.tensor_scalar(nb_s, nb_i, SLOTS.bit_length() - 1, None, ALU.logical_shift_right))
            V.memset(zero, 0.0)
            link(V.tensor_copy(nb, nb_s))
            link(V.tensor_tensor_scan(ends, nb, zero, 0.0, ALU.add, ALU.add))
            link(V.tensor_scalar(small[:, 288:320], ends, part_iota[:], None, ALU.is_le))
            dve.wait_ge(S["bdn_zero"], 1)
            V.tensor_reduce(pad_v[:, 0, 0:1], small[:, 288:320], AX.X, ALU.add).then_inc(S["cnt_ok"], 1)
            V.memset(bounds[:, 0:1], 0)
            link(V.tensor_copy(bounds[0:1, 1:E + 1], ends[0:1, :]))
            link(V.tensor_tensor(nb, ends, nb, ALU.subtract))
            for h in range(TH):
                ins = V.scalar_tensor_tensor(places[:, h, :], nb, float(SLOTS), ps[:, TB, E * h:E * (h + 1)], ALU.mult, ALU.add)
            link(ins)
            link(V.scalar_tensor_tensor(places[:], places[:], 1.0, sel, ALU.add, ALU.mult))
            link(V.tensor_scalar(places[:], places[:], -1.0, None, ALU.add))
            dve.wait_ge(S["cnt_ps"], 1)
            V.tensor_scalar(expert_of[:], ps[0:1, HB, 0:P], E - 1.0, None, ALU.min).then_inc(S["bounds_ok"], 1)

            def pick(base, column):
                for h in range(TH):
                    ins = V.tensor_scalar(onehot[:, h], slot_iota[:], base, column(h), ALU.add, ALU.is_equal)
                return ins
            pick(block_base[:, 0:1], lambda h: places[:, h, 0:1]).then_inc(S["onehot0"], 1)
            V.tensor_copy(bias_sel[:], ident[:, 0:1].to_broadcast([P, SLOTS])).then_inc(S["sel_bias"], 1)
            V.memset(back[:], 0.0).then_inc(S["back_sb"], 1)
            dve.wait_ge(S["lpart_ps"], 1)
            V.memset(y_sb[:, 0:512], 0.0).then_inc(S["y0_sb"], 1)
            V.memset(y_sb[:, 512:D], 0.0).then_inc(S["y1_sb"], 1)
            dve.wait_ge(S["rows0_ps"], 1)
            dve.wait_ge(S["gpad_ps"], 1)
            dve.wait_ge(S["bounds_ok"], 1)
            dve.wait_ge(S["onehot0"], 1)
            n_blocks = dve.value_load(bounds[0:1, E:E + 1], min_val=1, max_val=MAXB)
            with dve.Fori(0, n_blocks) as g:
                now = g + 1
                e = dve.value_load(expert_of[0:1, bass.ds(g, 1)], min_val=0, max_val=E - 1)
                e_next = dve.value_load(expert_of[0:1, bass.ds(now, 1)], min_val=0, max_val=E - 1)
                for h in range(TH):
                    ins = V.tensor_scalar(gated[:, h, :], onehot[:, h].rearrange("p j s -> p (j s)"), gates[:, h, bass.ds(e, 1)], None, ALU.mult)
                ins.then_inc(S["gated_ok"], 1)
                dve.wait_ge(S["gated_ok"], now)
                pick(block_base[:, bass.ds(now, 1)], lambda h: places[:, h, bass.ds(e_next, 1)]).then_inc(S["onehot_ok"], 1)
                dve.wait_ge(S["h_ps"], now)
                V.tensor_scalar(glu[:], half(HB, 0), SWIGLU_LIMIT, None, ALU.min).then_inc(S["glu_ok"], 1)
                V.tensor_scalar(lin[:], half(HB, 1), SWIGLU_LIMIT, -SWIGLU_LIMIT, ALU.min, ALU.max).then_inc(S["lin_ok"], 1)
                dve.wait_ge(S["lin_ok"], now)
                V.scalar_tensor_tensor(lin[:], lin[:], 1.0, glu[:], ALU.add, ALU.mult).then_inc(S["scaled"], 1)
                dve.wait_ge(S["scaled"], now)
                dve.wait_ge(S["sig_ok"], now)
                V.tensor_tensor(lin[:], lin[:], sig[:], ALU.mult).then_inc(S["act_ok"], 1)
                V.tensor_copy(bias_sel[:], ident[:, bass.ds(e_next, 1)].to_broadcast([P, SLOTS])).then_inc(S["sel_bias"], 1)
                dve.wait_ge(S["act_t_ps"], now)
                V.tensor_copy(act_t[:], half(TB, 0).rearrange("p (b s) -> p b s", b=2)).then_inc(S["act_t_sb"], 1)
                dve.wait_ge(S["y_ps"], now)
                V.tensor_copy(y_sb[:, 512:D], ps[:, Y1, :]).then_inc(S["y1_sb"], 1)
            dve.wait_ge(S["acc_done"], 1)
            dve.wait_ge(S["ln2_in"], 32)
            layer_norm(late[:, 0, :], late[:, 1, :], S["fin_var"], S["fin_rstd"], S["fin_ok"])

        @block.tensor
        def _(pe):
            T = nc.tensor
            pe.wait_ge(S["consts"], 1)
            pe.wait_ge(S["params_loaded"], 16 * 6)
            T.transpose(ps[:, HB, 0:P], params_in, ident[:]).then_inc(S["params_t"], 1)
            pe.wait_ge(S["x_in"], 16)
            for k in range(KT):
                for h in range(TH):
                    ins = T.transpose(ps[:, k // 2, 256 * (k % 2) + P * h:256 * (k % 2) + P * (h + 1)], xs[:, h, P * k:P * (k + 1)], ident[:])
                if k % 2:
                    ins.then_inc(S["xt_ps"], 1)

            def project(i, banks):
                pe.wait_ge(w_in_s[i], 16)
                for c in range(CT):
                    for k in range(KT):
                        ins = T.matmul(half(banks[c // 2], c % 2), w_piece[:, piece_slot[i], k, P * c:P * (c + 1)], turned[:, k, :],
                                       start=(k == 0), stop=(k == KT - 1))
                ins.then_inc(S["proj"], 1)
            pe.wait_ge(S["xt_sb_act"], 2)
            pe.wait_ge(S["xt_sb_dve"], 2)
            pe.wait_ge(S["params_ok"], 1)
            project(RX, (4, 5))
            project(RG, (6, 7))
            pe.wait_ge(S["u_ok"], 2)
            pe.wait_ge(S["bd_in"], 64)
            pe.wait_ge(S["rx_sb"], 2)
            pe.wait_ge(S["rg_sb"], 2)
            for n, wt in enumerate((wr_bd, wi_bd)):
                for i in range(CT):
                    ins = T.matmul(half(4 + 2 * n + i // 2, i % 2), wt[:, i, :], u[:, i, :], start=True, stop=True)
                ins.then_inc(S["gates_ps"], 1)
            project(CC, (0, 1))
            project(CH, (2, 3))
            pe.wait_ge(S["gate_sb"], CT)
            project(CB, (4, 5))
            pe.wait_ge(S["wout_in"], 16)
            pe.wait_ge(S["mix_lru"], 1)
            pe.wait_ge(S["cc_sb"], 2)
            pe.wait_ge(S["ch_used"], 2)
            order = list(range(CT, KT)) + list(range(CT))
            for n, k in enumerate(order):
                if k == 0:
                    pe.wait_ge(S["mix_conv"], 2)
                for h in range(TH):
                    for c in range(2):
                        ins = T.matmul(ps[:, 2 * h + c, :], mix[:, k, P * h:P * (h + 1)], w_out_v[:, k, 512 * c:512 * c + 512],
                                       start=(n == 0), stop=(n == KT - 1))
            ins.then_inc(S["out_ps"], 1)
            pe.wait_ge(S["x1_ok"], 2)
            pe.wait_ge(S["gate_sb"], 2 * CT)
            for k in range(KT):
                for h in range(TH):
                    ins = T.transpose(ps[:, 4 + k // 2, 256 * (k % 2) + P * h:256 * (k % 2) + P * (h + 1)], xs[:, h, P * k:P * (k + 1)], ident[:])
                if k % 2:
                    ins.then_inc(S["x1t_ps"], 1)
            pe.wait_ge(S["x1t_act"], 2)
            pe.wait_ge(S["x1t_dve"], 3)
            pe.wait_ge(S["small_in"], 32)
            per = KT // GROUPS
            for m in range(per):
                for j in range(GROUPS):
                    ins = T.matmul(ps[SLOTS * j:SLOTS * (j + 1), HB, 0:SEQ], wr[:, per * j + m, :], x1t[:, per * j + m, :],
                                   start=(m == 0), stop=(m == per - 1))
            ins.then_inc(S["lpart_ps"], 1)
            pe.wait_ge(S["lpart_sb"], 1)
            for h in range(TH):
                ins = T.matmul(ps[:, Y0, E * h:E * (h + 1)], glu[:, P * h:P * (h + 1)], stack_ident[:], start=True, stop=True)
            ins.then_inc(S["logits_ps"], 1)
            pe.wait_ge(S["sel_ok"], 1)
            sel_bf = bias_sel[:].bitcast(BF16).rearrange("p (h e) -> p h e", h=TH)
            T.matmul(ps[:, TB, 0:E], before[:], sel_bf[:, 0, :], start=True, stop=True)
            T.matmul(ps[:, TB, E:2 * E], ones_bf[:], sel_bf[:, 0, :], start=True, stop=False)
            T.matmul(ps[:, TB, E:2 * E], before[:], sel_bf[:, 1, :], start=False, stop=True)
            T.matmul(ps[:, TB, 2 * E:3 * E], ones_bf[:], sel_bf[:, 0, :], start=True, stop=False)
            T.matmul(ps[:, TB, 2 * E:3 * E], ones_bf[:], sel_bf[:, 1, :], start=False, stop=True).then_inc(S["pos_ps"], 1)
            pe.wait_ge(S["cnt_ok"], 1)
            T.transpose(ps[:, HB, 0:P], pad_v[:, 0, :], ident[:]).then_inc(S["cnt_ps"], 1)
            pe.wait_ge(S["gates_ok"], TH)
            for h in range(TH):
                ins = T.transpose(ps[0:E, Y1, P * h:P * (h + 1)], gates[:, h, :], ident[:])
            ins.then_inc(S["gpad_ps"], 1)
            pe.wait_ge(S["gpad_sb"], 1)
            pe.wait_ge(S["bdn_in"], 16)
            for h in range(TH):
                for c in range(2):
                    ins = T.matmul(ps[:, 2 * h + c, :], gatesT_v[0:E, P * h:P * (h + 1)], b_dn_v[0:E, 512 * c:512 * c + 512],
                                   start=True, stop=False, skip_group_check=True)
            ins.then_inc(S["acc_started"], 1)

            def gather():
                for h in range(TH):
                    for j in range(GROUPS):
                        ins = T.matmul(ps[SLOTS * j:SLOTS * (j + 1), Y0, 0:QF], onehot[:, h, 0, :], xs[:, h, QF * j:QF * (j + 1)],
                                       start=(h == 0), stop=(h == TH - 1))
                return ins

            def turn(bank, src):
                for b in range(2):
                    ins = T.transpose(ps[:, bank, P * b:P * (b + 1)], src[:, P * b:P * (b + 1)], ident[:])
                return ins

            def combine():
                for h in range(TH):
                    for c in range(2):
                        ins = T.matmul(ps[:, 2 * h + c, :], back[:, P * h:P * (h + 1)], y_sb[:, 512 * c:512 * c + 512],
                                       start=False, stop=False, skip_group_check=True)
                return ins

            pe.wait_ge(S["onehot0"], 1)
            gather().then_inc(S["rows0_ps"], 1)
            pe.wait_ge(S["rows0_sb"], 1)
            pe.wait_ge(S["bounds_ok"], 1)
            turn(HB, rows).then_inc(S["rows0t_ps"], 1)
            pe.wait_ge(S["bgu_in"], 16)
            with pe.Fori(0, E // 2) as pair:
                loads = (pair + 1) * 16
                for b in range(2):
                    first = pe.value_load(bounds[0:1, bass.ds(pair * 2 + b, 1)], min_val=0, max_val=MAXB - 1)
                    end = pe.value_load(bounds[0:1, bass.ds(pair * 2 + b + 1, 1)], min_val=1, max_val=MAXB)
                    dn_loads = (pair * 2 + (b + 1)) * 16
                    with pe.Fori(first, end) as g:
                        now = g + 1
                        after = g + 2
                        pe.wait_ge(S["rows_t_ok"], now)
                        pe.wait_ge(S["sel_bias"], now)
                        for j in range(GROUPS):
                            T.matmul(ps[SLOTS * j:SLOTS * (j + 1), HB, :], bias_sel[:],
                                     b_gu.rearrange("p (two n) -> p two n", two=2)[:, :, QF * j:QF * (j + 1)], start=True, stop=False)
                        for c in range(GC):
                            pe.wait_ge(gu_in[b][c], loads)
                            for k in range(GK * c, GK * (c + 1)):
                                for j in range(GROUPS):
                                    ins = T.matmul(ps[SLOTS * j:SLOTS * (j + 1), HB, :],
                                                   rows_t[:, k % 2, SLOTS * (k // 2):SLOTS * (k // 2 + 1)],
                                                   gu_buf[:, b, k, :].rearrange("p (two n) -> p two n", two=2)[:, :, QF * j:QF * (j + 1)],
                                                   start=False, stop=(k == KT - 1))
                            if c < GC - 1:
                                ins.then_inc(gu_used[c], 1)
                        ins.then_inc(S["h_ps"], 1)
                        pe.wait_ge(S["onehot_ok"], now)
                        pe.wait_ge(S["y0_sb"], now)
                        gather().then_inc(S["rows_ps"], 1)
                        pe.wait_ge(S["y1_sb"], now)
                        pe.wait_ge(S["back_sb"], now)
                        combine()
                        pe.wait_ge(S["gated_ok"], now)
                        turn(Y1, gated[:].rearrange("p h n -> p (h n)")).then_inc(S["back_ps"], 1)
                        pe.wait_ge(S["act_ok"], now)
                        turn(TB, lin).then_inc(S["act_t_ps"], 1)
                        pe.wait_ge(S["rows_sb"], now)
                        turn(HB, rows).then_inc(S["rows_t_ps"], 1)
                        pe.wait_ge(S["back_sb"], after)
                        pe.wait_ge(S["act_t_sb"], now)
                        for m in range(DC):
                            pe.wait_ge(dn_in[m], dn_loads)
                            for c in range(2):
                                for j in range(GROUPS):
                                    ins = T.matmul(ps[SLOTS * j:SLOTS * (j + 1), Y0 + c, :], act_t[:, m, SLOTS * j:SLOTS * (j + 1)],
                                                   dn_buf[:, m, j, 512 * c:512 * c + 512], start=(m == 0), stop=(m == DC - 1))
                            if m == 0:
                                ins.then_inc(dn_used[0], 1)
                        ins.then_inc(S["y_ps"], 1)
            n_blocks = pe.value_load(bounds[0:1, E:E + 1], min_val=1, max_val=MAXB)
            pe.wait_ge(S["y0_sb"], n_blocks + 1)
            pe.wait_ge(S["y1_sb"], n_blocks + 1)
            combine().then_inc(S["acc_done"], 1)


_INS = ["x", "w_in", "conv_w", "lru_conv_w", "lru_conv_b", "w_rgate", "b_rgate", "w_igate", "b_igate", "lru_lambda", "w_out",
        "ln1_g", "ln1_b", "w_router", "b_router", "w_gate_up", "b_gate_up", "w_down", "b_down", "ln2_g", "ln2_b"]


def kernel(**inputs):
    import numpy as _np
    import concourse.bacc as _bacc
    from concourse.bass_utils import run_bass_kernel_spmd as _run

    nc = _bacc.Bacc("TRN2", target_bir_lowering=False, num_devices=1)
    arrays, args = {}, []
    for name in _INS:
        a = _np.ascontiguousarray(inputs[name])
        arrays[f"in_{name}_dram"] = a
        args.append(nc.dram_tensor(f"in_{name}_dram", a.shape, mybir.dt.from_np(a.dtype), kind="ExternalInput").ap())
    shape = _np.shape(inputs["x"])
    args.append(nc.dram_tensor("out_0_dram", shape, F32, kind="ExternalOutput").ap())
    trunk(nc, *args)
    r = _run(nc, [arrays], core_ids=[0])
    return r.results[0]["out_0_dram"]
```

```python
from contextlib import ExitStack

import concourse.bass as bass
from concourse import mybir

F32 = mybir.dt.float32
BF16 = mybir.dt.bfloat16
I32 = mybir.dt.int32
U32 = mybir.dt.uint32
ALU = mybir.AluOpType
ACT = mybir.ActivationFunctionType
AX = mybir.AxisListType

P = 128
SLOTS = 32
GROUPS = P // SLOTS
LRU_C = 8.0
SWIGLU_LIMIT = 7.0
SWIGLU_ALPHA = 1.702
LN_EPS = 1e-5
TOP_K = 4
GELU_IN = 2.0 * (2.0 / 3.141592653589793) ** 0.5
GELU_CUBE = 0.044715
TINY = 1e-35


def trunk(nc, x, w_in, conv_w, lru_conv_w, lru_conv_b, w_rgate, b_rgate, w_igate, b_igate, lru_lambda, w_out,
          ln1_g, ln1_b, w_router, b_router, w_gate_up, b_gate_up, w_down, b_down, ln2_g, ln2_b, out):
    SEQ, D = x.shape[1], x.shape[2]
    KT = D // P
    TH = SEQ // P
    C = D // 2
    CT = C // P
    E = w_router.shape[2]
    F = w_down.shape[2]
    HD = w_rgate.shape[2]
    CW = conv_w.shape[1]
    LW = lru_conv_w.shape[1]
    alpha = (2.0 * x.shape[0]) ** 0.25
    assert (SEQ, D, E, F) == (256, 1024, 32, 1024) and 2 * HD == P
    QF = F // GROUPS
    MAXB = TOP_K * SEQ // SLOTS + E
    GC = 4
    DC = 2
    GK = KT // GC
    PIECE = 512
    RX, RG, CC, CH, CB = range(5)
    COLS = {RX: 3 * C, RG: 3 * C + C, CC: C, CH: 2 * C, CB: 0}

    with ExitStack() as ctx:
        def sb(name, shape, dt=F32):
            return ctx.enter_context(nc.sbuf_tensor(name, shape, dt))

        def sem(name):
            return ctx.enter_context(nc.semaphore(name))

        gu_buf = sb("gu_buf", [P, 2, KT, 2 * F])
        dn_buf = sb("dn_buf", [P, DC, GROUPS, D])
        xs = sb("xs", [P, TH, D])
        turned = sb("turned", [P, KT, SEQ])
        mix = sb("mix", [P, KT, SEQ])
        late = sb("late", [P, 2, D])
        wr = sb("wr", [P, KT, E])
        ident = sb("ident", [P, P])
        stack_ident = sb("stack_ident", [P, E])
        slot_iota = sb("slot_iota", [P, GROUPS, SLOTS])
        before = sb("before", [P, P], BF16)
        ones_bf = sb("ones_bf", [P, P], BF16)
        block_base = sb("block_base", [P, MAXB + 1])
        part_iota = sb("part_iota", [P, 1])
        b_rout = sb("b_rout", [P, E])
        onehot = sb("onehot", [P, TH, GROUPS, SLOTS])
        gated = sb("gated", [P, TH, P])
        back = sb("back", [P, TH * P])
        rows = sb("rows", [P, QF])
        rows_t = sb("rows_t", [P, 2, P])
        glu = sb("glu", [P, QF])
        lin = sb("lin", [P, QF])
        sig = sb("sig", [P, QF])
        act_t = sb("act_t", [P, 2, P])
        bias_sel = sb("bias_sel", [P, SLOTS])
        places = sb("places", [P, TH, E])
        gates = sb("gates", [P, TH, E])
        small = sb("small", [P, 384])
        bounds = sb("bounds", [1, E + 1], I32)
        expert_of = sb("expert_of", [1, P], I32)
        gates_t = sb("gates_t", [E, TH * P])

        w_piece = gu_buf[:, 1].rearrange("p (s a) (b n) -> p s (a b) n", s=4, n=PIECE)
        piece_slot = {RX: 0, RG: 1, CC: 2, CH: 3, CB: 0}
        w_out_v = gu_buf[:, 1, 2:6].rearrange("p a (b n) -> p (a b) n", n=D)
        scratch = dn_buf[:].rearrange("p m j n -> p (m j n)")
        at = [0]

        def take(n):
            at[0] += n
            return scratch[:, at[0] - n:at[0]]
        rx = take(CT * (SEQ + LW - 1)).rearrange("p (i t) -> p i t", i=CT)
        cv = take(CT * (SEQ + CW - 1)).rearrange("p (i t) -> p i t", i=CT)
        u, rgate, igate, rec, gel = [take(CT * SEQ).rearrange("p (i t) -> p i t", i=CT) for _ in range(5)]
        params_in = take(P)
        gel2 = rx[:, :, 0:SEQ]
        wr_bd = late[:, 0, 0:CT * P].rearrange("p (i n) -> p i n", i=CT)
        wi_bd = late[:, 1, 0:CT * P].rearrange("p (i n) -> p i n", i=CT)
        y_sb = mix[:].rearrange("p k t -> p (k t)")[:, 0:D]
        b_dn = mix[:].rearrange("p k t -> p (k t)")[0:E, D:2 * D]
        x1t = mix[:].rearrange("p k (h t) -> p h k t", h=TH)
        closed = act_t[:, 0, :]
        scaled_ident = act_t[:, 1, :]
        b_gu = turned[:].rearrange("p k t -> p (k t)")
        prm = small[:, 0:64]
        N_PRM = CT * (LW + CW + 4)
        off_lw, off_cw, off_lb, off_br, off_bi, off_lam = [CT * v for v in (0, LW, LW + CW, LW + CW + 1, LW + CW + 2, LW + CW + 3)]

        ps = ctx.enter_context(nc.psum_tensor("ps", [P, 8, 512], F32))
        HB, Y0, Y1, TB = 4, 5, 6, 7

        def half(bank, n):
            return ps[:, bank, 256 * n:256 * n + 256]

        S = {n: sem(n) for n in (
            "x_in0", "x_in1", "params_in", "matrices_in", "router_in", "wout_in0", "wout_in1", "ln1_in", "ln2_in", "bgu_in", "bdn_in", "stored",
            "ident_ok", "consts", "params_zero", "matrices_zero", "bgu_zero", "closed_zero",
            "params_ps", "params_ok", "xt_ps", "xt_act", "xt_dve", "proj", "rx_sb", "rg_sb", "cc_sb", "u_ok", "lam_ok", "lam_sig",
            "softplus_ok", "gates_ps", "gate_sb", "tanh_ok", "tanh_kept", "sqrt_ok", "gelu_in", "gelu_sig", "ch_used",
            "mix_lru", "mix_conv", "out_ps",
            "var_ok", "rstd_ok", "x1_ok", "x1t_ps", "x1t_act", "x1t_dve", "lpart_ps", "lpart_sb", "logits_ps", "exp_in", "exp_ok",
            "gates_ok", "gates_t_ps", "gates_t_ok", "sel_ok", "rank_ps", "closed_ok", "closed_ps", "bounds_ok", "experts_ok", "acc_started",
            "onehot0", "rows0_ps", "rows0_sb", "rows0_t_ps",
            "rows_t_ok", "sel_bias", "h_ps", "onehot_ok", "y0_sb", "y1_sb", "back_sb", "rows_ps", "gated_ok", "back_ps", "act_ok",
            "act_t_ps", "rows_sb", "rows_t_ps", "act_t_sb", "y_ps", "glu_ok", "lin_ok", "scaled_ok", "sig_ok",
            "acc_done", "fin_var", "fin_rstd", "fin_ok", "dve_link", "pool_link")}
        w_in_s = [sem(f"w_in{i}") for i in range(5)]
        rx2_in = sem("rx2_in")
        gu_in = [[sem(f"gu_in{b}{c}") for c in range(GC)] for b in range(2)]
        dn_in = [sem(f"dn_in{c}") for c in range(DC)]
        gu_used = [sem(f"gu_used{c}") for c in range(GC - 1)] + [S["h_ps"]]
        dn_used = [sem("dn_used0"), S["y_ps"]]

        gu_src = w_gate_up[0].rearrange("e (k p) n -> e p k n", p=P)
        dn_src = w_down[0].rearrange("e (j m p) n -> e m p j n", p=P, m=DC)
        w_in_src = w_in[0].rearrange("(k p) n -> p k n", p=P)
        w_out_src = w_out[0].rearrange("(k p) n -> p k n", p=P)
        x_src = x[0].rearrange("(h p) d -> p h d", p=P)
        out_dst = out[0].rearrange("(h p) d -> p h d", p=P)

        block = ctx.enter_context(nc.Block())

        @block.sync
        def _(sp):
            def load_gu(e, b, c):
                return sp.dma_start(gu_buf[:, b, GK * c:GK * (c + 1), :], gu_src[e][:, GK * c:GK * (c + 1), :]).then_inc(gu_in[b][c], 16)

            def load_dn(e, c):
                return sp.dma_start(dn_buf[:, c], dn_src[e, c]).then_inc(dn_in[c], 16)

            for h in range(TH):
                sp.dma_start(xs[:, h, :], x_src[:, h, :]).then_inc(S[f"x_in{h}"], 16)
            sp.wait_ge(S["params_zero"], 1)
            row = 0
            for src, n in ((lru_conv_w[0].rearrange("k (i p) -> (k i) p", p=P), LW), (conv_w[0].rearrange("k (i p) -> (k i) p", p=P), CW),
                           (lru_conv_b[0].rearrange("(i p) -> i p", p=P), 1), (b_rgate[0].rearrange("(i p) -> i p", p=P), 1),
                           (b_igate[0].rearrange("(i p) -> i p", p=P), 1), (lru_lambda[0].rearrange("(i p) -> i p", p=P), 1)):
                sp.dma_start(params_in[row:row + n * CT, :], src).then_inc(S["params_in"], 16)
                row += n * CT
            half_p = PIECE // 2
            sp.dma_start(w_piece[:, piece_slot[RX], :, 0:half_p], w_in_src[:, :, COLS[RX]:COLS[RX] + half_p]).then_inc(w_in_s[RX], 16)
            sp.dma_start(w_piece[:, piece_slot[RX], :, half_p:], w_in_src[:, :, COLS[RX] + half_p:COLS[RX] + PIECE]).then_inc(rx2_in, 16)
            for i in (RG, CC, CH):
                sp.dma_start(w_piece[:, piece_slot[i]], w_in_src[:, :, COLS[i]:COLS[i] + PIECE]).then_inc(w_in_s[i], 16)
            sp.wait_ge(S["proj"], 1)
            sp.dma_start(w_piece[:, piece_slot[CB]], w_in_src[:, :, COLS[CB]:COLS[CB] + PIECE]).then_inc(w_in_s[CB], 16)
            for c in range(2):
                load_gu(0, 0, c)
            sp.wait_ge(S["proj"], 2)
            sp.dma_start(w_out_v[:, 0:CT], w_out_src[:, CT:KT]).then_inc(S["wout_in0"], 16)
            for c in range(2, GC):
                load_gu(0, 0, c)
            sp.wait_ge(S["gates_ps"], 2)
            sp.dma_start(late[:, 0, :], ln1_g[0:1, :].to_broadcast([P, D])).then_inc(S["ln1_in"], 16)
            sp.dma_start(late[:, 1, :], ln1_b[0:1, :].to_broadcast([P, D])).then_inc(S["ln1_in"], 16)
            sp.wait_ge(S["proj"], 3)
            sp.dma_start(w_out_v[:, CT:KT], w_out_src[:, 0:CT]).then_inc(S["wout_in1"], 16)
            sp.wait_ge(S["proj"], 4)
            load_gu(1, 1, 3)
            sp.wait_ge(S["proj"], 5)
            load_gu(1, 1, 0)
            sp.wait_ge(S["mix_lru"], 1)
            sp.wait_ge(S["mix_conv"], 2)
            for c in range(DC):
                load_dn(0, c)
            sp.wait_ge(S["bgu_zero"], 1)
            sp.dma_start(b_gu[0:E, :], b_gate_up[0]).then_inc(S["bgu_in"], 16)
            sp.wait_ge(S["out_ps"], 2)
            for c in (1, 2):
                load_gu(1, 1, c)
            sp.wait_ge(S["x1_ok"], 2)
            sp.dma_start(late[:, 0, :], ln2_g[0:1, :].to_broadcast([P, D])).then_inc(S["ln2_in"], 16)
            sp.dma_start(late[:, 1, :], ln2_b[0:1, :].to_broadcast([P, D])).then_inc(S["ln2_in"], 16)
            sp.wait_ge(S["lpart_ps"], 1)
            sp.dma_start(b_dn, b_down[0]).then_inc(S["bdn_in"], 16)
            sp.wait_ge(S["bounds_ok"], 1)

            def stream_gu(e, b):
                before_last = sp.value_load(bounds[0:1, bass.ds(e - 1, 1)], min_val=1, max_val=MAXB)
                for c in range(GC):
                    sp.wait_ge(gu_used[c], before_last)
                    sp.dma_start(gu_buf[:, b, GK * c:GK * (c + 1), :],
                                 gu_src[bass.ds(e, 1)].rearrange("o p k n -> p (o k) n")[:, GK * c:GK * (c + 1), :]).then_inc(gu_in[b][c], 16)

            def stream_dn(e):
                last = sp.value_load(bounds[0:1, bass.ds(e, 1)], min_val=1, max_val=MAXB)
                for c in range(DC):
                    sp.wait_ge(dn_used[c], last)
                    sp.dma_start(dn_buf[:, c], dn_src[bass.ds(e, 1), c].rearrange("o p j n -> p (o j) n")).then_inc(dn_in[c], 16)
            stream_gu(2, 0)
            stream_dn(1)
            with sp.Fori(1, E // 2 - 1) as pair:
                stream_dn(pair * 2)
                stream_gu(pair * 2 + 1, 1)
                stream_dn(pair * 2 + 1)
                stream_gu(pair * 2 + 2, 0)
            stream_dn(E - 2)
            stream_gu(E - 1, 1)
            stream_dn(E - 1)
            for h in range(TH):
                for c in range(2):
                    sp.wait_ge(S["fin_ok"], 2 * h + c + 1)
                    sp.dma_start(out_dst[:, h, 512 * c:512 * c + 512], xs[:, h, 512 * c:512 * c + 512]).then_inc(S["stored"], 16)
            sp.wait_ge(S["stored"], 16 * 2 * TH)

        @block.gpsimd
        def _(pool):
            links = [0]

            def link(ins):
                links[0] += 1
                ins.then_inc(S["pool_link"], 1)
                pool.wait_ge(S["pool_link"], links[0])

            nc.gpsimd.memset(params_in, 0.0).then_inc(S["params_zero"], 1)
            link(nc.gpsimd.memset(ident[:], 0.0))
            nc.gpsimd.affine_select(out=ident[:], in_=ident[:], compare_op=ALU.not_equal, fill=1.0, base=0,
                                    pattern=[[-1, P]], channel_multiplier=1).then_inc(S["ident_ok"], 1)
            nc.gpsimd.memset(late[:, 0, 0:CT * P], 0.0).then_inc(S["matrices_zero"], 1)
            nc.gpsimd.memset(late[:, 1, 0:CT * P], 0.0).then_inc(S["matrices_zero"], 1)
            nc.gpsimd.iota(slot_iota[:], pattern=[[0, GROUPS], [1, SLOTS]], base=0, channel_multiplier=0,
                           allow_small_or_imprecise_dtypes=True)
            nc.gpsimd.iota(block_base[:], pattern=[[SLOTS, MAXB + 1]], base=0, channel_multiplier=0,
                           allow_small_or_imprecise_dtypes=True)
            nc.gpsimd.iota(part_iota[:], pattern=[[0, 1]], base=0, channel_multiplier=1,
                           allow_small_or_imprecise_dtypes=True)
            link(nc.gpsimd.memset(gated[:, 0, :], 1.0))
            link(nc.gpsimd.affine_select(out=gated[:, 1, :], in_=gated[:, 0, :], compare_op=ALU.is_gt, fill=0.0, base=0,
                                         pattern=[[1, P]], channel_multiplier=-1))
            nc.gpsimd.tensor_copy(before[:], gated[:, 1, :])
            nc.gpsimd.tensor_copy(ones_bf[:], gated[:, 0, :])
            pool.wait_ge(S["ident_ok"], 1)
            nc.gpsimd.tensor_scalar(scaled_ident, ident[:], alpha, None, ALU.mult)
            nc.gpsimd.memset(closed, 0.0).then_inc(S["closed_zero"], 1)
            nc.gpsimd.memset(small[:, 380:382], -0.5).then_inc(S["consts"], 1)
            nc.gpsimd.memset(back[:], 0.0).then_inc(S["back_sb"], 1)
            pool.wait_ge(S["proj"], 5)
            nc.gpsimd.memset(b_gu, 0.0).then_inc(S["bgu_zero"], 1)
            for h in range(TH):
                pool.wait_ge(S["var_ok"], h + 1)
                nc.gpsimd.tensor_tensor(small[:, 374 + h:375 + h], small[:, 370 + h:371 + h], small[:, 380:381], ALU.pow).then_inc(S["rstd_ok"], 1)
            pool.wait_ge(S["lpart_ps"], 1)
            nc.gpsimd.memset(y_sb[:, 0:512], 0.0).then_inc(S["y0_sb"], 1)
            nc.gpsimd.memset(y_sb[:, 512:D], 0.0).then_inc(S["y1_sb"], 1)
            for h in range(TH):
                pool.wait_ge(S["fin_var"], h + 1)
                nc.gpsimd.tensor_tensor(small[:, 374 + h:375 + h], small[:, 370 + h:371 + h], small[:, 380:381], ALU.pow).then_inc(S["fin_rstd"], 1)

        @block.scalar
        def _(act):
            for b in (0, 2):
                act.wait_ge(S["xt_ps"], b + 1)
                nc.scalar.copy(turned[:, 2 * b:2 * b + 2, :], ps[:, b, :].rearrange("p (k t) -> p k t", k=2)).then_inc(S["xt_act"], 1)
            act.wait_ge(S["matrices_zero"], 2)
            for dst, src in ((wr_bd, w_rgate), (wi_bd, w_igate)):
                heads = src[0].rearrange("(i two) r c -> two r i c", two=2)
                for s in range(2):
                    act.dma_start(dst[HD * s:HD * (s + 1), :, HD * s:HD * (s + 1)], heads[s]).then_inc(S["matrices_in"], 16)
            act.dma_start(wr[:], w_router[0].rearrange("(k p) e -> p k e", p=P)).then_inc(S["router_in"], 16)
            act.dma_start(b_rout[:], b_router[0:1, :].to_broadcast([P, E])).then_inc(S["router_in"], 16)

            act.wait_ge(S["lam_ok"], 1)
            nc.scalar.activation(small[:, 80:84], small[:, 76:80], ACT.Sigmoid).then_inc(S["lam_sig"], 1)
            act.wait_ge(S["proj"], 1)
            for b in range(2):
                nc.scalar.copy(rx[:, 2 * b:2 * b + 2, LW - 1:], ps[:, 4 + b, :].rearrange("p (i t) -> p i t", i=2)).then_inc(S["rx_sb"], 1)
            act.wait_ge(S["proj"], 2)
            for b in range(2):
                nc.scalar.copy(gel[:, 2 * b:2 * b + 2, :], ps[:, 6 + b, :].rearrange("p (i t) -> p i t", i=2)).then_inc(S["rg_sb"], 1)
            for n, (dst, off) in enumerate(((rgate, off_br), (igate, off_bi))):
                act.wait_ge(S["gates_ps"], n + 1)
                act.wait_ge(S["params_ok"], 1)
                for i in range(CT):
                    nc.scalar.activation(dst[:, i, :], half(4 + 2 * n + i // 2, i % 2), ACT.Sigmoid,
                                         bias=prm[:, off + i:off + i + 1]).then_inc(S["gate_sb"], 1)
            act.wait_ge(S["softplus_ok"], 1)
            act.wait_ge(S["gate_sb"], CT)
            for i in range(CT):
                nc.scalar.activation(rgate[:, i, :], rgate[:, i, :], ACT.Tanh, scale=small[:, 64 + i:65 + i]).then_inc(S["tanh_ok"], 1)
            act.wait_ge(S["gelu_in"], 1)
            nc.scalar.activation(gel2, gel2, ACT.Sigmoid, scale=GELU_IN).then_inc(S["gelu_sig"], 1)
            act.wait_ge(S["tanh_kept"], 1)
            nc.scalar.activation(rgate, rgate, ACT.Sqrt).then_inc(S["sqrt_ok"], 1)
            act.wait_ge(S["proj"], 3)
            for b in range(2):
                nc.scalar.copy(cv[:, 2 * b:2 * b + 2, CW - 1:], ps[:, b, :].rearrange("p (i t) -> p i t", i=2)).then_inc(S["cc_sb"], 1)
            for n in range(3):
                act.wait_ge(S["x1t_ps"], n + 1)
                nc.scalar.copy(x1t[:, n // 2, CT * (n % 2):CT * (n % 2 + 1), :],
                               ps[:, 4 + n, :].rearrange("p (k t) -> p k t", k=CT)).then_inc(S["x1t_act"], 1)
            act.wait_ge(S["lpart_ps"], 1)
            nc.scalar.copy(glu[:], half(HB, 0)).then_inc(S["lpart_sb"], 1)
            act.wait_ge(S["exp_in"], 1)
            nc.scalar.activation(small[:, 128:192], small[:, 64:128], ACT.Sigmoid).then_inc(S["exp_ok"], 1)
            act.wait_ge(S["rows0_ps"], 1)
            nc.scalar.copy(rows[:], half(Y0, 0)).then_inc(S["rows0_sb"], 1)
            act.wait_ge(S["rows0_t_ps"], 1)
            nc.scalar.copy(rows_t[:], half(Y0, 0).rearrange("p (b s) -> p b s", b=2)).then_inc(S["rows_t_ok"], 1)
            act.wait_ge(S["gates_t_ps"], 1)
            nc.scalar.copy(gates_t[:], ps[0:E, TB, 0:SEQ]).then_inc(S["gates_t_ok"], 1)

            act.wait_ge(S["bounds_ok"], 1)
            n_blocks = act.value_load(bounds[0:1, E:E + 1], min_val=1, max_val=MAXB)
            with act.Fori(0, n_blocks) as g:
                now = g + 1
                act.wait_ge(S["glu_ok"], now)
                nc.scalar.activation(sig[:], glu[:], ACT.Sigmoid, scale=SWIGLU_ALPHA).then_inc(S["sig_ok"], 1)
                act.wait_ge(S["rows_ps"], now)
                nc.scalar.copy(rows[:], half(Y0, 0)).then_inc(S["rows_sb"], 1)
                act.wait_ge(S["back_ps"], now)
                nc.scalar.copy(back[:], half(Y1, 0)).then_inc(S["back_sb"], 1)
                act.wait_ge(S["rows_t_ps"], now)
                nc.scalar.copy(rows_t[:], half(HB, 0).rearrange("p (b s) -> p b s", b=2)).then_inc(S["rows_t_ok"], 1)
                act.wait_ge(S["y_ps"], now)
                nc.scalar.copy(y_sb[:, 0:512], ps[:, Y0, :]).then_inc(S["y0_sb"], 1)

        @block.vector
        def _(dve):
            V = nc.vector
            links = [0]

            def link(ins):
                links[0] += 1
                ins.then_inc(S["dve_link"], 1)
                dve.wait_ge(S["dve_link"], links[0])

            V.memset(rx[:, :, 0:LW - 1], 0.0)
            V.memset(cv[:, :, 0:CW - 1], 0.0)
            for b in (1, 3):
                dve.wait_ge(S["xt_ps"], b + 1)
                V.tensor_copy(turned[:, 2 * b:2 * b + 2, :], ps[:, b, :].rearrange("p (k t) -> p k t", k=2)).then_inc(S["xt_dve"], 1)
            dve.wait_ge(S["params_ps"], 1)
            V.tensor_copy(prm, ps[:, TB, 0:64]).then_inc(S["params_ok"], 1)
            dve.wait_ge(S["consts"], 1)
            V.tensor_reduce(stack_ident[:], ident[:].rearrange("p (j e) -> p e j", e=E), AX.X, ALU.add)
            lam = prm[:, off_lam:off_lam + CT]
            t = [small[:, 72 + CT * i:72 + CT * (i + 1)] for i in range(6)]
            dve.wait_ge(S["params_ok"], 1)
            link(V.tensor_scalar(t[0], lam, -1.0, None, ALU.mult))
            link(V.tensor_tensor(t[1], t[0], lam, ALU.min))
            V.tensor_scalar(t[5], t[0], 0.0, None, ALU.max).then_inc(S["lam_ok"], 1)
            dve.wait_ge(S["lam_sig"], 1)
            link(V.tensor_scalar(t[3], t[2], -1.0, 2.0, ALU.mult, ALU.add))
            link(V.reciprocal(t[4], t[3]))
            link(V.tensor_tensor(t[0], t[2], t[4], ALU.mult))
            link(V.tensor_tensor(t[1], t[0], t[0], ALU.mult))
            link(V.memset(t[3], 1.0 / 17))
            for n in range(7, -1, -1):
                link(V.tensor_tensor(t[4], t[3], t[1], ALU.mult))
                link(V.tensor_scalar(t[3], t[4], 1.0 / (2 * n + 1), None, ALU.add))
            link(V.scalar_tensor_tensor(t[2], t[0], 2.0, t[3], ALU.mult, ALU.mult))
            link(V.tensor_tensor(t[4], t[2], t[5], ALU.add))
            V.tensor_scalar(small[:, 64:64 + CT], t[4], LRU_C / 2, None, ALU.mult).then_inc(S["softplus_ok"], 1)
            for b in range(2):
                dve.wait_ge(S["rx_sb"], b + 1)
                for k in range(LW - 1, -1, -1):
                    for i in (2 * b, 2 * b + 1):
                        w = prm[:, off_lw + CT * k + i:off_lw + CT * k + i + 1]
                        if k == LW - 1:
                            ins = V.tensor_scalar(u[:, i, :], rx[:, i, k:k + SEQ], w, prm[:, off_lb + i:off_lb + i + 1], ALU.mult, ALU.add)
                        else:
                            ins = V.scalar_tensor_tensor(u[:, i, :], rx[:, i, k:k + SEQ], w, u[:, i, :], ALU.mult, ALU.add)
                    if k:
                        link(ins)
                ins.then_inc(S["u_ok"], 1)
            dve.wait_ge(S["rg_sb"], 2)
            dve.wait_ge(S["u_ok"], 2)
            link(V.tensor_tensor(gel2, gel, gel, ALU.mult))
            link(V.tensor_scalar(gel2, gel2, GELU_CUBE, 1.0, ALU.mult, ALU.add))
            V.tensor_tensor(gel2, gel2, gel, ALU.mult).then_inc(S["gelu_in"], 1)
            dve.wait_ge(S["tanh_ok"], CT)
            link(V.tensor_scalar(rec, rgate, 1.0, None, ALU.add))
            V.tensor_scalar(rgate, rgate, TINY, None, ALU.max).then_inc(S["tanh_kept"], 1)
            link(V.reciprocal(rec, rec))
            dve.wait_ge(S["gate_sb"], 2 * CT)
            link(V.tensor_tensor(igate, igate, u, ALU.mult))
            dve.wait_ge(S["sqrt_ok"], 1)
            link(V.scalar_tensor_tensor(rgate, rgate, 2.0, rec, ALU.mult, ALU.mult))
            link(V.tensor_tensor(igate, igate, rgate, ALU.mult))
            link(V.tensor_scalar(rec, rec, 2.0, -1.0, ALU.mult, ALU.add))
            for i in range(CT):
                ins = V.tensor_tensor_scan(u[:, i, :], rec[:, i, :], igate[:, i, :], 0.0, ALU.mult, ALU.add)
            link(ins)
            dve.wait_ge(S["gelu_sig"], 1)
            link(V.tensor_tensor(gel, gel, gel2, ALU.mult))
            V.tensor_tensor(mix[:, CT:KT, :], u, gel, ALU.mult).then_inc(S["mix_lru"], 1)
            dve.wait_ge(S["proj"], 4)
            dve.wait_ge(S["cc_sb"], 2)
            for b in range(2):
                V.tensor_tensor(cv[:, 2 * b:2 * b + 2, CW - 1:], cv[:, 2 * b:2 * b + 2, CW - 1:],
                                ps[:, 2 + b, :].rearrange("p (i t) -> p i t", i=2), ALU.mult).then_inc(S["ch_used"], 1)
            dve.wait_ge(S["ch_used"], 2)
            for k in range(CW):
                for i in range(CT):
                    w = prm[:, off_cw + CT * k + i:off_cw + CT * k + i + 1]
                    if k == 0:
                        ins = V.tensor_scalar(mix[:, i, :], cv[:, i, k:k + SEQ], w, None, ALU.mult)
                    else:
                        ins = V.scalar_tensor_tensor(mix[:, i, :], cv[:, i, k:k + SEQ], w, mix[:, i, :], ALU.mult, ALU.add)
                link(ins)
            dve.wait_ge(S["proj"], 5)
            for b in range(2):
                V.tensor_tensor(mix[:, 2 * b:2 * b + 2, :], mix[:, 2 * b:2 * b + 2, :],
                                ps[:, 4 + b, :].rearrange("p (i t) -> p i t", i=2), ALU.mult).then_inc(S["mix_conv"], 1)

            stats = small[:, 336:360].rearrange("p (h c s) -> p h c s", h=TH, c=2)
            mv = small[:, 360:364].rearrange("p (h s) -> p h s", h=TH)

            def norm_stats(h, g_ap, var_sem):
                for c in range(2):
                    ins = V.bn_stats(stats[:, h, c, :], ps[:, 2 * h + c, :])
                link(ins)
                link(V.bn_aggr(mv[:, h, :], stats[:, h, :, :]))
                V.tensor_scalar(small[:, 370 + h:371 + h], mv[:, h, 1:2], LN_EPS, None, ALU.add).then_inc(var_sem, 1)
                for c in range(2):
                    v = ps[:, 2 * h + c, :]
                    ins = V.scalar_tensor_tensor(v, v, mv[:, h, 0:1], g_ap[:, 512 * c:512 * c + 512], ALU.subtract, ALU.mult)
                link(ins)

            def norm_scale(h, c, b_ap):
                return V.scalar_tensor_tensor(xs[:, h, 512 * c:512 * c + 512], ps[:, 2 * h + c, :], small[:, 374 + h:375 + h],
                                              b_ap[:, 512 * c:512 * c + 512], ALU.mult, ALU.add)

            dve.wait_ge(S["ln1_in"], 32)
            for h in range(TH):
                dve.wait_ge(S["out_ps"], h + 1)
                for c in range(2):
                    v = ps[:, 2 * h + c, :]
                    ins = V.scalar_tensor_tensor(v, xs[:, h, 512 * c:512 * c + 512], alpha, v, ALU.mult, ALU.add)
                link(ins)
                norm_stats(h, late[:, 0, :], S["var_ok"])
                dve.wait_ge(S["rstd_ok"], h + 1)
                for c in range(2):
                    ins = norm_scale(h, c, late[:, 1, :])
                ins.then_inc(S["x1_ok"], 1)
            dve.wait_ge(S["x1t_ps"], 4)
            V.tensor_copy(x1t[:, 1, CT:KT, :], ps[:, 7, :].rearrange("p (k t) -> p k t", k=CT)).then_inc(S["x1t_dve"], 1)
            lg = small[:, 0:64].rearrange("p (h e) -> p h e", h=TH)
            shifted = small[:, 64:128].rearrange("p (h e) -> p h e", h=TH)
            sg = small[:, 128:192].rearrange("p (h e) -> p h e", h=TH)
            sel = small[:, 192:256].rearrange("p (h e) -> p h e", h=TH)
            ex = small[:, 256:320].rearrange("p (h e) -> p h e", h=TH)
            top = small[:, 320:336].rearrange("p (h k) -> p h k", h=TH)
            idx = small[:, 336:352].bitcast(U32).rearrange("p (h k) -> p h k", h=TH)
            idxf = small[:, 352:368].rearrange("p (h k) -> p h k", h=TH)
            total = small[:, 368:370]
            eye_row = slot_iota[:, 0, :]
            dve.wait_ge(S["logits_ps"], 1)
            dve.wait_ge(S["router_in"], 32)
            dve.wait_ge(S["x1_ok"], 2)
            link(V.tensor_tensor(lg, ps[:, Y0, 0:TH * E].rearrange("p (h e) -> p h e", h=TH),
                                 b_rout[:].unsqueeze(1).to_broadcast([P, TH, E]), ALU.add))
            for h in range(TH):
                ins = V.max(top[:, h, :], lg[:, h, :])
            link(ins)
            for h in range(TH):
                ins = V.max_index(idx[:, h, :], top[:, h, :], lg[:, h, :])
            ins.then_inc(S["dve_link"], 1)
            links[0] += 1
            V.tensor_tensor(shifted, lg, top[:, :, 0:1].to_broadcast([P, TH, E]), ALU.subtract).then_inc(S["exp_in"], 1)
            dve.wait_ge(S["dve_link"], links[0])
            link(V.tensor_copy(idxf, idx))
            hits = onehot[:].rearrange("p h j s -> p (h j s)").rearrange("p (h e k) -> p h e k", h=TH, k=TOP_K)
            link(V.tensor_tensor(hits, eye_row.unsqueeze(1).unsqueeze(3).to_broadcast([P, TH, E, TOP_K]),
                                 idxf[:, :, 0:TOP_K].unsqueeze(2).to_broadcast([P, TH, E, TOP_K]), ALU.is_equal))
            link(V.tensor_reduce(sel, hits, AX.X, ALU.add))
            sel_bf = bias_sel[:].bitcast(BF16).rearrange("p (h e) -> p h e", h=TH)
            V.tensor_copy(sel_bf, sel).then_inc(S["sel_ok"], 1)
            dve.wait_ge(S["exp_ok"], 1)
            link(V.tensor_scalar(ex, sg, -1.0, 1.0, ALU.mult, ALU.add))
            link(V.reciprocal(ex, ex))
            link(V.tensor_tensor(ex, ex, sg, ALU.mult))
            dve.wait_ge(S["rank_ps"], 1)
            rank = ps[:, TB, 0:TH * E].rearrange("p (h e) -> p h e", h=TH)
            link(V.scalar_tensor_tensor(places[:], rank, 1.0, sel, ALU.add, ALU.mult))
            link(V.tensor_scalar(small[:, 372:374], places[:, :, 0], -1.0, None, ALU.add))
            for h in range(TH):
                ins = V.tensor_scalar(onehot[:, h], slot_iota[:], small[:, 372 + h:373 + h], None, ALU.is_equal)
            ins.then_inc(S["onehot0"], 1)
            V.tensor_copy(bias_sel[:], ident[:, 0:1].to_broadcast([P, SLOTS])).then_inc(S["sel_bias"], 1)
            nb_i = small[:, 64:96].bitcast(I32)
            nb_s = small[:, 96:128].bitcast(I32)
            nb, ends, zero = small[:, 320:352], small[:, 64:96], small[:, 128:160]
            cnt = ps[:, TB, 2 * E:3 * E]
            link(V.tensor_scalar(nb_i, cnt, 1.0, SLOTS - 1.0, ALU.max, ALU.add))
            V.memset(zero, 0.0)
            V.memset(bounds[:, 0:1], 0)
            link(V.tensor_scalar(nb_s, nb_i, SLOTS.bit_length() - 1, None, ALU.logical_shift_right))
            link(V.tensor_copy(nb, nb_s))
            link(V.tensor_tensor_scan(ends, nb, zero, 0.0, ALU.add, ALU.add))
            V.tensor_copy(bounds[0:1, 1:E + 1], ends[0:1, :]).then_inc(S["bounds_ok"], 1)
            link(V.tensor_scalar(small[:, 96:128], ends, part_iota[:], None, ALU.is_le))
            dve.wait_ge(S["closed_zero"], 1)
            V.tensor_reduce(closed[:, 0:1], small[:, 96:128], AX.X, ALU.add).then_inc(S["closed_ok"], 1)
            link(V.tensor_tensor(ex, ex, sel, ALU.mult))
            link(V.tensor_reduce(total, ex, AX.X, ALU.add))
            link(V.reciprocal(total, total))
            V.tensor_tensor(gates[:], ex, total.unsqueeze(2).to_broadcast([P, TH, E]), ALU.mult).then_inc(S["gates_ok"], 1)
            dve.wait_ge(S["closed_ps"], 1)
            V.tensor_scalar(expert_of[:], ps[0:1, HB, 0:P], E - 1.0, None, ALU.min).then_inc(S["experts_ok"], 1)
            dve.wait_ge(S["experts_ok"], 1)
            link(V.tensor_tensor(nb, ends, nb, ALU.subtract))
            link(V.scalar_tensor_tensor(sel, nb.unsqueeze(1).to_broadcast([P, TH, E]), float(SLOTS), sel, ALU.mult, ALU.mult))
            link(V.scalar_tensor_tensor(places[:], places[:], -1.0, sel, ALU.add, ALU.add))

            def pick(base, column):
                for h in range(TH):
                    ins = V.tensor_scalar(onehot[:, h], slot_iota[:], base, column(h), ALU.add, ALU.is_equal)
                return ins
            dve.wait_ge(S["rows0_ps"], 1)
            n_blocks = dve.value_load(bounds[0:1, E:E + 1], min_val=1, max_val=MAXB)
            with dve.Fori(0, n_blocks) as g:
                now = g + 1
                e = dve.value_load(expert_of[0:1, bass.ds(g, 1)], min_val=0, max_val=E - 1)
                e_next = dve.value_load(expert_of[0:1, bass.ds(now, 1)], min_val=0, max_val=E - 1)
                for h in range(TH):
                    ins = V.tensor_scalar(gated[:, h, :], onehot[:, h].rearrange("p j s -> p (j s)"), gates[:, h, bass.ds(e, 1)], None, ALU.mult)
                ins.then_inc(S["gated_ok"], 1)
                dve.wait_ge(S["gated_ok"], now)
                pick(block_base[:, bass.ds(now, 1)], lambda h: places[:, h, bass.ds(e_next, 1)]).then_inc(S["onehot_ok"], 1)
                dve.wait_ge(S["h_ps"], now)
                V.tensor_scalar(glu[:], half(HB, 0), SWIGLU_LIMIT, None, ALU.min).then_inc(S["glu_ok"], 1)
                V.tensor_scalar(lin[:], half(HB, 1), SWIGLU_LIMIT, -SWIGLU_LIMIT, ALU.min, ALU.max).then_inc(S["lin_ok"], 1)
                dve.wait_ge(S["lin_ok"], now)
                V.scalar_tensor_tensor(lin[:], lin[:], 1.0, glu[:], ALU.add, ALU.mult).then_inc(S["scaled_ok"], 1)
                dve.wait_ge(S["scaled_ok"], now)
                dve.wait_ge(S["sig_ok"], now)
                V.tensor_tensor(lin[:], lin[:], sig[:], ALU.mult).then_inc(S["act_ok"], 1)
                V.tensor_copy(bias_sel[:], ident[:, bass.ds(e_next, 1)].to_broadcast([P, SLOTS])).then_inc(S["sel_bias"], 1)
                dve.wait_ge(S["act_t_ps"], now)
                V.tensor_copy(act_t[:], half(TB, 0).rearrange("p (b s) -> p b s", b=2)).then_inc(S["act_t_sb"], 1)
                dve.wait_ge(S["y_ps"], now)
                V.tensor_copy(y_sb[:, 512:D], ps[:, Y1, :]).then_inc(S["y1_sb"], 1)
            dve.wait_ge(S["ln2_in"], 32)
            for h in range(TH):
                dve.wait_ge(S["acc_done"], h + 1)
                norm_stats(h, late[:, 0, :], S["fin_var"])
            for h in range(TH):
                dve.wait_ge(S["fin_rstd"], h + 1)
                for c in range(2):
                    norm_scale(h, c, late[:, 1, :]).then_inc(S["fin_ok"], 1)

        @block.tensor
        def _(pe):
            T = nc.tensor
            pe.wait_ge(S["ident_ok"], 1)
            for h in range(TH):
                pe.wait_ge(S[f"x_in{h}"], 16)
                for k in range(KT):
                    ins = T.transpose(ps[:, k // 2, 256 * (k % 2) + P * h:256 * (k % 2) + P * (h + 1)], xs[:, h, P * k:P * (k + 1)], ident[:])
                    if k % 2 and h == TH - 1:
                        ins.then_inc(S["xt_ps"], 1)

            def project(i, banks):
                pe.wait_ge(w_in_s[i], 16)
                for c in range(CT):
                    if i == RX and c == CT // 2:
                        pe.wait_ge(S["params_in"], 16 * 6)
                        T.transpose(ps[:, TB, 0:P], params_in, ident[:]).then_inc(S["params_ps"], 1)
                        pe.wait_ge(rx2_in, 16)
                    for k in range(KT):
                        ins = T.matmul(half(banks[c // 2], c % 2), w_piece[:, piece_slot[i], k, P * c:P * (c + 1)], turned[:, k, :],
                                       start=(k == 0), stop=(k == KT - 1))
                ins.then_inc(S["proj"], 1)
            pe.wait_ge(S["xt_act"], 2)
            pe.wait_ge(S["xt_dve"], 2)
            project(RX, (4, 5))
            pe.wait_ge(S["params_ok"], 1)
            project(RG, (6, 7))
            pe.wait_ge(S["u_ok"], 2)
            pe.wait_ge(S["matrices_in"], 64)
            pe.wait_ge(S["rx_sb"], 2)
            pe.wait_ge(S["rg_sb"], 2)
            for n, wt in enumerate((wr_bd, wi_bd)):
                for i in range(CT):
                    ins = T.matmul(half(4 + 2 * n + i // 2, i % 2), wt[:, i, :], u[:, i, :], start=True, stop=True)
                ins.then_inc(S["gates_ps"], 1)
            project(CC, (0, 1))
            project(CH, (2, 3))
            pe.wait_ge(S["gate_sb"], CT)
            project(CB, (4, 5))
            pe.wait_ge(S["mix_lru"], 1)
            pe.wait_ge(S["wout_in0"], 16)
            pe.wait_ge(S["cc_sb"], 2)
            pe.wait_ge(S["ch_used"], 2)

            def mixer_out(n, h, k):
                for c in range(2):
                    ins = T.matmul(ps[:, 2 * h + c, :], mix[:, k, P * h:P * (h + 1)], w_out_v[:, n, 512 * c:512 * c + 512],
                                   start=(n == 0), stop=(n == KT - 1))
                return ins
            for n in range(CT):
                for h in range(TH):
                    mixer_out(n, h, CT + n)
            pe.wait_ge(S["mix_conv"], 2)
            pe.wait_ge(S["wout_in1"], 16)
            for h in range(TH):
                for n in range(CT):
                    ins = mixer_out(CT + n, h, n)
                ins.then_inc(S["out_ps"], 1)
            def start_sum(h):
                for c in range(2):
                    T.matmul(ps[:, 2 * h + c, :], scaled_ident, xs[:, h, 512 * c:512 * c + 512],
                             start=True, stop=False, skip_group_check=True)
            pe.wait_ge(S["gate_sb"], 2 * CT)
            for h in range(TH):
                pe.wait_ge(S["x1_ok"], h + 1)
                for k in range(KT):
                    ins = T.transpose(ps[:, 4 + 2 * h + k // CT, P * (k % CT):P * (k % CT + 1)], xs[:, h, P * k:P * (k + 1)], ident[:])
                    if k % CT == CT - 1:
                        ins.then_inc(S["x1t_ps"], 1)
                if h == 0:
                    start_sum(h)
            pe.wait_ge(S["x1t_act"], 3)
            pe.wait_ge(S["x1t_dve"], 1)
            pe.wait_ge(S["router_in"], 32)
            per = KT // GROUPS
            for m in range(per):
                for j in range(GROUPS):
                    ins = T.matmul(ps[SLOTS * j:SLOTS * (j + 1), HB, 0:SEQ], wr[:, per * j + m, :], x1t[:, :, per * j + m, :],
                                   start=(m == 0), stop=(m == per - 1))
            ins.then_inc(S["lpart_ps"], 1)
            pe.wait_ge(S["lpart_sb"], 1)
            for h in range(TH):
                ins = T.matmul(ps[:, Y0, E * h:E * (h + 1)], glu[:, P * h:P * (h + 1)], stack_ident[:], start=True, stop=True)
            ins.then_inc(S["logits_ps"], 1)
            start_sum(1)
            pe.wait_ge(S["sel_ok"], 1)
            sel_bf = bias_sel[:].bitcast(BF16).rearrange("p (h e) -> p h e", h=TH)
            T.matmul(ps[:, TB, 0:E], before[:], sel_bf[:, 0, :], start=True, stop=True)
            T.matmul(ps[:, TB, E:2 * E], ones_bf[:], sel_bf[:, 0, :], start=True, stop=False)
            T.matmul(ps[:, TB, E:2 * E], before[:], sel_bf[:, 1, :], start=False, stop=True)
            T.matmul(ps[:, TB, 2 * E:3 * E], ones_bf[:], sel_bf[:, 0, :], start=True, stop=False)
            T.matmul(ps[:, TB, 2 * E:3 * E], ones_bf[:], sel_bf[:, 1, :], start=False, stop=True).then_inc(S["rank_ps"], 1)

            def gather():
                for h in range(TH):
                    for j in range(GROUPS):
                        ins = T.matmul(ps[SLOTS * j:SLOTS * (j + 1), Y0, 0:QF], onehot[:, h, 0, :], xs[:, h, QF * j:QF * (j + 1)],
                                       start=(h == 0), stop=(h == TH - 1))
                return ins

            def turn(bank, src):
                for b in range(2):
                    ins = T.transpose(ps[:, bank, P * b:P * (b + 1)], src[:, P * b:P * (b + 1)], ident[:])
                return ins

            def combine():
                last = []
                for h in range(TH):
                    for c in range(2):
                        ins = T.matmul(ps[:, 2 * h + c, :], back[:, P * h:P * (h + 1)], y_sb[:, 512 * c:512 * c + 512],
                                       start=False, stop=False, skip_group_check=True)
                    last.append(ins)
                return last

            pe.wait_ge(S["onehot0"], 1)
            gather().then_inc(S["rows0_ps"], 1)
            pe.wait_ge(S["closed_ok"], 1)
            T.transpose(ps[:, HB, 0:P], closed, ident[:]).then_inc(S["closed_ps"], 1)
            pe.wait_ge(S["rows0_sb"], 1)
            for b in range(2):
                ins = T.transpose(ps[:, Y0, P * b:P * (b + 1)], rows[:, P * b:P * (b + 1)], ident[:])
            ins.then_inc(S["rows0_t_ps"], 1)
            pe.wait_ge(S["gates_ok"], 1)
            for h in range(TH):
                ins = T.transpose(ps[0:E, TB, P * h:P * (h + 1)], gates[:, h, :], ident[:])
            ins.then_inc(S["gates_t_ps"], 1)
            pe.wait_ge(S["bounds_ok"], 1)
            pe.wait_ge(S["bgu_in"], 16)
            pe.wait_ge(S["experts_ok"], 1)
            def pair_of_experts(pair):
                loads = (pair + 1) * 16
                for b in range(2):
                    first = pe.value_load(bounds[0:1, bass.ds(pair * 2 + b, 1)], min_val=0, max_val=MAXB - 1)
                    end = pe.value_load(bounds[0:1, bass.ds(pair * 2 + b + 1, 1)], min_val=1, max_val=MAXB)
                    dn_loads = (pair * 2 + (b + 1)) * 16
                    with pe.Fori(first, end) as g:
                        now = g + 1
                        after = g + 2
                        pe.wait_ge(S["rows_t_ok"], now)
                        pe.wait_ge(S["sel_bias"], now)
                        for j in range(GROUPS):
                            T.matmul(ps[SLOTS * j:SLOTS * (j + 1), HB, :], bias_sel[:],
                                     b_gu.rearrange("p (two n) -> p two n", two=2)[:, :, QF * j:QF * (j + 1)], start=True, stop=False)
                        for c in range(GC):
                            pe.wait_ge(gu_in[b][c], loads)
                            for k in range(GK * c, GK * (c + 1)):
                                for j in range(GROUPS):
                                    ins = T.matmul(ps[SLOTS * j:SLOTS * (j + 1), HB, :],
                                                   rows_t[:, k % 2, SLOTS * (k // 2):SLOTS * (k // 2 + 1)],
                                                   gu_buf[:, b, k, :].rearrange("p (two n) -> p two n", two=2)[:, :, QF * j:QF * (j + 1)],
                                                   start=False, stop=(k == KT - 1))
                            if c < GC - 1:
                                ins.then_inc(gu_used[c], 1)
                        ins.then_inc(S["h_ps"], 1)
                        pe.wait_ge(S["onehot_ok"], now)
                        pe.wait_ge(S["y0_sb"], now)
                        gather().then_inc(S["rows_ps"], 1)
                        pe.wait_ge(S["y1_sb"], now)
                        pe.wait_ge(S["back_sb"], now)
                        combine()
                        pe.wait_ge(S["gated_ok"], now)
                        turn(Y1, gated[:].rearrange("p h n -> p (h n)")).then_inc(S["back_ps"], 1)
                        pe.wait_ge(S["act_ok"], now)
                        turn(TB, lin).then_inc(S["act_t_ps"], 1)
                        pe.wait_ge(S["rows_sb"], now)
                        turn(HB, rows).then_inc(S["rows_t_ps"], 1)
                        pe.wait_ge(S["back_sb"], after)
                        pe.wait_ge(S["act_t_sb"], now)
                        for m in range(DC):
                            pe.wait_ge(dn_in[m], dn_loads)
                            for c in range(2):
                                for j in range(GROUPS):
                                    ins = T.matmul(ps[SLOTS * j:SLOTS * (j + 1), Y0 + c, :], act_t[:, m, SLOTS * j:SLOTS * (j + 1)],
                                                   dn_buf[:, m, j, 512 * c:512 * c + 512], start=(m == 0), stop=(m == DC - 1))
                            if m == 0:
                                ins.then_inc(dn_used[0], 1)
                        ins.then_inc(S["y_ps"], 1)

            with pe.Fori(0, E // 2 - 1) as pair:
                pair_of_experts(pair)
            pe.wait_ge(S["bdn_in"], 16)
            pe.wait_ge(S["gates_t_ok"], 1)
            for h in range(TH):
                for c in range(2):
                    T.matmul(ps[:, 2 * h + c, :], gates_t[:, P * h:P * (h + 1)], b_dn[:, 512 * c:512 * c + 512],
                             start=False, stop=False, skip_group_check=True)
            with pe.Fori(E // 2 - 1, E // 2) as pair:
                pair_of_experts(pair)
            n_blocks = pe.value_load(bounds[0:1, E:E + 1], min_val=1, max_val=MAXB)
            pe.wait_ge(S["y0_sb"], n_blocks + 1)
            pe.wait_ge(S["y1_sb"], n_blocks + 1)
            for ins in combine():
                ins.then_inc(S["acc_done"], 1)


_INS = ["x", "w_in", "conv_w", "lru_conv_w", "lru_conv_b", "w_rgate", "b_rgate", "w_igate", "b_igate", "lru_lambda", "w_out",
        "ln1_g", "ln1_b", "w_router", "b_router", "w_gate_up", "b_gate_up", "w_down", "b_down", "ln2_g", "ln2_b"]


def kernel(**inputs):
    import numpy as _np
    import concourse.bacc as _bacc
    from concourse.bass_utils import run_bass_kernel_spmd as _run

    nc = _bacc.Bacc("TRN2", target_bir_lowering=False, num_devices=1)
    arrays, args = {}, []
    for name in _INS:
        a = _np.ascontiguousarray(inputs[name])
        arrays[f"in_{name}_dram"] = a
        args.append(nc.dram_tensor(f"in_{name}_dram", a.shape, mybir.dt.from_np(a.dtype), kind="ExternalInput").ap())
    shape = _np.shape(inputs["x"])
    args.append(nc.dram_tensor("out_0_dram", shape, F32, kind="ExternalOutput").ap())
    trunk(nc, *args)
    r = _run(nc, [arrays], core_ids=[0])
    return r.results[0]["out_0_dram"]
```

```python
from contextlib import ExitStack

import concourse.bass as bass
from concourse import mybir

F32 = mybir.dt.float32
BF16 = mybir.dt.bfloat16
I32 = mybir.dt.int32
U32 = mybir.dt.uint32
ALU = mybir.AluOpType
ACT = mybir.ActivationFunctionType
AX = mybir.AxisListType

P = 128
SLOTS = 32
GROUPS = P // SLOTS
LRU_C = 8.0
SWIGLU_LIMIT = 7.0
SWIGLU_ALPHA = 1.702
LN_EPS = 1e-5
TOP_K = 4
GELU_IN = 2.0 * (2.0 / 3.141592653589793) ** 0.5
GELU_CUBE = 0.044715
TINY = 1e-35


def trunk(nc, x, w_in, conv_w, lru_conv_w, lru_conv_b, w_rgate, b_rgate, w_igate, b_igate, lru_lambda, w_out,
          ln1_g, ln1_b, w_router, b_router, w_gate_up, b_gate_up, w_down, b_down, ln2_g, ln2_b, out):
    SEQ, D = x.shape[1], x.shape[2]
    KT = D // P
    TH = SEQ // P
    C = D // 2
    CT = C // P
    E = w_router.shape[2]
    F = w_down.shape[2]
    HD = w_rgate.shape[2]
    CW = conv_w.shape[1]
    LW = lru_conv_w.shape[1]
    alpha = (2.0 * x.shape[0]) ** 0.25
    assert (SEQ, D, E, F) == (256, 1024, 32, 1024) and 2 * HD == P
    QF = F // GROUPS
    MAXB = TOP_K * SEQ // SLOTS + E
    GC = 4
    DC = 2
    GK = KT // GC
    PIECE = 512
    RX, RG, CC, CH, CB = range(5)
    COLS = {RX: 3 * C, RG: 3 * C + C, CC: C, CH: 2 * C, CB: 0}

    with ExitStack() as ctx:
        def sb(name, shape, dt=F32):
            return ctx.enter_context(nc.sbuf_tensor(name, shape, dt))

        def sem(name):
            return ctx.enter_context(nc.semaphore(name))

        gu_buf = sb("gu_buf", [P, 2, KT, 2 * F])
        dn_buf = sb("dn_buf", [P, DC, GROUPS, D])
        xs = sb("xs", [P, TH, D])
        turned = sb("turned", [P, KT, SEQ])
        mix = sb("mix", [P, KT, SEQ])
        late = sb("late", [P, 2, D])
        wr = sb("wr", [P, KT, E])
        ident = sb("ident", [P, P])
        stack_ident = sb("stack_ident", [P, E])
        slot_iota = sb("slot_iota", [P, GROUPS, SLOTS])
        before = sb("before", [P, P], BF16)
        ones_bf = sb("ones_bf", [P, P], BF16)
        block_base = sb("block_base", [P, MAXB + 1])
        part_iota = sb("part_iota", [P, 1])
        b_rout = sb("b_rout", [P, E])
        onehot = sb("onehot", [P, TH, GROUPS, SLOTS])
        gated = sb("gated", [P, TH, P])
        back = sb("back", [P, TH * P])
        rows = sb("rows", [P, QF])
        rows_t = sb("rows_t", [P, 2, P])
        glu = sb("glu", [P, QF])
        lin = sb("lin", [P, QF])
        sig = sb("sig", [P, QF])
        act_t = sb("act_t", [P, 2, P])
        bias_sel = sb("bias_sel", [P, GROUPS, SLOTS])
        places = sb("places", [P, TH, E])
        gates = sb("gates", [P, TH, E])
        small = sb("small", [P, 384])
        bounds = sb("bounds", [1, E + 1], I32)
        expert_of = sb("expert_of", [1, P], I32)

        w_piece = gu_buf[:, 1].rearrange("p (s a) (b n) -> p s (a b) n", s=4, n=PIECE)
        piece_slot = {RX: 0, RG: 1, CC: 2, CH: 3, CB: 0}
        w_out_v = gu_buf[:, 1, 2:6].rearrange("p a (b n) -> p (a b) n", n=D)
        scratch = dn_buf[:].rearrange("p m j n -> p (m j n)")
        at = [0]

        def take(n):
            at[0] += n
            return scratch[:, at[0] - n:at[0]]
        rx = take(CT * (SEQ + LW - 1)).rearrange("p (i t) -> p i t", i=CT)
        cv = take(CT * (SEQ + CW - 1)).rearrange("p (i t) -> p i t", i=CT)
        u, rgate, igate, rec, gel = [take(CT * SEQ).rearrange("p (i t) -> p i t", i=CT) for _ in range(5)]
        params_in = take(P)
        gel2 = rx[:, :, 0:SEQ]
        wr_bd = late[:, 0, 0:CT * P].rearrange("p (i n) -> p i n", i=CT)
        wi_bd = late[:, 1, 0:CT * P].rearrange("p (i n) -> p i n", i=CT)
        x1t = mix[:].rearrange("p k (h t) -> p h k t", h=TH)
        closed = act_t[:, 0, :]
        scaled_ident = act_t[:, 1, :]
        turned_v = turned[:].rearrange("p k t -> p (k t)")
        mix_v = mix[:].rearrange("p k t -> p (k t)")
        y_sb = mix_v[:, 0:D]
        b_dn = mix_v[0:E, D:2 * D]
        b_gu = turned_v[:, 0:2 * QF]
        gates_t = turned_v[0:E, 2 * QF:2 * QF + SEQ]
        dn_extra = [late[:, 0, :], late[:, 1, :], mix_v[:, D:2 * D], turned_v[:, D:2 * D]]
        ident_v = ident[:].rearrange("p (j e) -> p j e", j=GROUPS)
        sel_bf = bias_sel[:].rearrange("p j s -> p (j s)")[:, 0:E].bitcast(BF16).rearrange("p (h e) -> p h e", h=TH)
        prm = small[:, 0:64]
        N_PRM = CT * (LW + CW + 4)
        off_lw, off_cw, off_lb, off_br, off_bi, off_lam = [CT * v for v in (0, LW, LW + CW, LW + CW + 1, LW + CW + 2, LW + CW + 3)]

        ps = ctx.enter_context(nc.psum_tensor("ps", [P, 8, 512], F32))
        HB, Y0, Y1, TB = 4, 5, 6, 7

        def half(bank, n):
            return ps[:, bank, 256 * n:256 * n + 256]

        S = {n: sem(n) for n in (
            "x_in0", "x_in1", "params_in", "matrices_in", "router_in", "wout_in0", "wout_in1", "ln1_in", "ln2_in", "bgu_in", "bdn_in", "extra_in", "stored",
            "ident_ok", "consts", "params_zero", "matrices_zero", "closed_zero",
            "params_ps", "params_ok", "xt_ps", "xt_act", "xt_dve", "proj", "rx_sb", "rg_sb", "cc_sb", "u_ok", "lam_ok", "lam_sig",
            "softplus_ok", "gates_ps", "gate_sb", "tanh_ok", "tanh_kept", "sqrt_ok", "gelu_in", "gelu_sig", "ch_used",
            "mix_lru", "mix_conv", "lru_out_ps", "out_ps",
            "var_ok", "centred", "rstd_ok", "x1_ok", "x1t_ps", "x1t_act", "x1t_dve", "lpart_ps", "lpart_sb", "logits_ps", "exp_in", "exp_ok",
            "gates_ok", "gates_t_ps", "gates_t_ok", "sel_ok", "rank_ps", "closed_ok", "closed_ps", "bounds_ok",
            "onehot0", "rows0_ps", "rows0_sb", "rows0_t_ps",
            "rows_t_ok", "sel_bias", "h_ps", "onehot_ok", "y0_sb", "y1_sb", "back_sb", "rows_ps", "gated_ok", "back_ps", "act_ok",
            "act_t_ps", "rows_sb", "rows_t_ps", "act_t_sb", "y0_ps", "y_ps", "glu_ok", "lin_ok", "scaled_ok", "sig_ok",
            "acc_done", "fin_var", "fin_centred", "fin_rstd", "fin_ok", "dve_link", "pool_link")}
        w_in_s = [sem(f"w_in{i}") for i in range(5)]
        rx2_in = sem("rx2_in")
        gu_in = [[sem(f"gu_in{b}{c}") for c in range(GC)] for b in range(2)]
        dn_in = [sem(f"dn_in{c}") for c in range(DC)]
        gu_used = [sem(f"gu_used{c}") for c in range(GC - 1)] + [S["h_ps"]]
        dn_used = [sem("dn_used0"), S["y_ps"]]

        gu_src = w_gate_up[0].rearrange("e (k p) n -> e p k n", p=P)
        dn_src = w_down[0].rearrange("e (j m p) n -> e m p j n", p=P, m=DC)
        w_in_src = w_in[0].rearrange("(k p) n -> p k n", p=P)
        w_out_src = w_out[0].rearrange("(k p) n -> p k n", p=P)
        x_src = x[0].rearrange("(h p) d -> p h d", p=P)
        out_dst = out[0].rearrange("(h p) d -> p h d", p=P)

        block = ctx.enter_context(nc.Block())

        @block.sync
        def _(sp):
            def load_gu(e, b, c):
                return sp.dma_start(gu_buf[:, b, GK * c:GK * (c + 1), :], gu_src[e][:, GK * c:GK * (c + 1), :]).then_inc(gu_in[b][c], 16)

            def load_dn(e, c):
                return sp.dma_start(dn_buf[:, c], dn_src[e, c]).then_inc(dn_in[c], 16)

            for h in range(TH):
                sp.dma_start(xs[:, h, :], x_src[:, h, :]).then_inc(S[f"x_in{h}"], 16)
            sp.wait_ge(S["params_zero"], 1)
            row = 0
            for src, n in ((lru_conv_w[0].rearrange("k (i p) -> (k i) p", p=P), LW), (conv_w[0].rearrange("k (i p) -> (k i) p", p=P), CW),
                           (lru_conv_b[0].rearrange("(i p) -> i p", p=P), 1), (b_rgate[0].rearrange("(i p) -> i p", p=P), 1),
                           (b_igate[0].rearrange("(i p) -> i p", p=P), 1), (lru_lambda[0].rearrange("(i p) -> i p", p=P), 1)):
                sp.dma_start(params_in[row:row + n * CT, :], src).then_inc(S["params_in"], 16)
                row += n * CT
            half_p = PIECE // 2
            sp.dma_start(w_piece[:, piece_slot[RX], :, 0:half_p], w_in_src[:, :, COLS[RX]:COLS[RX] + half_p]).then_inc(w_in_s[RX], 16)
            sp.dma_start(w_piece[:, piece_slot[RX], :, half_p:], w_in_src[:, :, COLS[RX] + half_p:COLS[RX] + PIECE]).then_inc(rx2_in, 16)
            for i in (RG, CC, CH):
                sp.dma_start(w_piece[:, piece_slot[i]], w_in_src[:, :, COLS[i]:COLS[i] + PIECE]).then_inc(w_in_s[i], 16)
            sp.wait_ge(S["proj"], 1)
            sp.dma_start(w_piece[:, piece_slot[CB]], w_in_src[:, :, COLS[CB]:COLS[CB] + PIECE]).then_inc(w_in_s[CB], 16)
            for c in range(2):
                load_gu(0, 0, c)
            sp.wait_ge(S["proj"], 2)
            sp.dma_start(w_out_v[:, 0:CT], w_out_src[:, CT:KT]).then_inc(S["wout_in0"], 16)
            for c in range(2, GC):
                load_gu(0, 0, c)
            sp.wait_ge(S["gates_ps"], 2)
            sp.dma_start(late[:, 0, :], ln1_g[0:1, :].to_broadcast([P, D])).then_inc(S["ln1_in"], 16)
            sp.dma_start(late[:, 1, :], ln1_b[0:1, :].to_broadcast([P, D])).then_inc(S["ln1_in"], 16)
            sp.wait_ge(S["proj"], 3)
            sp.dma_start(w_out_v[:, CT:KT], w_out_src[:, 0:CT]).then_inc(S["wout_in1"], 16)
            sp.wait_ge(S["proj"], 4)
            load_gu(1, 1, 3)
            sp.wait_ge(S["proj"], 5)
            load_gu(1, 1, 0)
            bias_src = b_gate_up[0].rearrange("e (two j n) -> j e two n", two=2, j=GROUPS)
            for j in range(GROUPS):
                sp.dma_start(b_gu[E * j:E * (j + 1), :].rearrange("p (two n) -> p two n", two=2), bias_src[j]).then_inc(S["bgu_in"], 16)

            def load_extra(j):
                sp.dma_start(dn_extra[j], dn_src[1, 0][:, j, :]).then_inc(S["extra_in"], 16)
            load_extra(3)
            sp.wait_ge(S["mix_lru"], 1)
            sp.wait_ge(S["mix_conv"], 2)
            for c in range(DC):
                load_dn(0, c)
            sp.wait_ge(S["lru_out_ps"], 1)
            load_gu(1, 1, 1)
            sp.wait_ge(S["out_ps"], 2 * TH)
            load_gu(1, 1, 2)
            sp.wait_ge(S["x1_ok"], 2 * TH)
            load_extra(0)
            load_extra(1)
            sp.wait_ge(S["lpart_ps"], 1)
            load_extra(2)
            sp.wait_ge(S["bounds_ok"], 1)

            def blocks_before(e):
                return sp.value_load(bounds[0:1, bass.ds(e, 1)], min_val=1, max_val=MAXB)

            def stream_gu(e, b):
                used = blocks_before(e - 1)
                for c in range(GC):
                    sp.wait_ge(gu_used[c], used)
                    sp.dma_start(gu_buf[:, b, GK * c:GK * (c + 1), :],
                                 gu_src[bass.ds(e, 1)].rearrange("o p k n -> p (o k) n")[:, GK * c:GK * (c + 1), :]).then_inc(gu_in[b][c], 16)

            def stream_dn_chunk(e, c, used):
                sp.wait_ge(dn_used[c], used)
                sp.dma_start(dn_buf[:, c], dn_src[bass.ds(e, 1), c].rearrange("o p j n -> p (o j) n")).then_inc(dn_in[c], 16)

            def stream_dn(e):
                used = blocks_before(e)
                for c in range(DC):
                    stream_dn_chunk(e, c, used)

            stream_gu(2, 0)
            after_0 = blocks_before(1)
            stream_dn_chunk(1, 1, after_0)
            stream_dn_chunk(2, 0, after_0)
            stream_dn_chunk(2, 1, blocks_before(2))
            sp.dma_start(b_dn, b_down[0]).then_inc(S["bdn_in"], 16)
            stream_gu(3, 1)
            with sp.Fori(2, E // 2) as pair:
                stream_dn(pair * 2 - 1)
                stream_gu(pair * 2, 0)
                stream_dn(pair * 2)
                stream_gu(pair * 2 + 1, 1)
            stream_dn(E - 1)
            sp.dma_start(late[:, 0, :], ln2_g[0:1, :].to_broadcast([P, D])).then_inc(S["ln2_in"], 16)
            sp.dma_start(late[:, 1, :], ln2_b[0:1, :].to_broadcast([P, D])).then_inc(S["ln2_in"], 16)
            for h in range(TH):
                for c in range(2):
                    sp.wait_ge(S["fin_ok"], 2 * h + c + 1)
                    sp.dma_start(out_dst[:, h, 512 * c:512 * c + 512], xs[:, h, 512 * c:512 * c + 512]).then_inc(S["stored"], 16)
            sp.wait_ge(S["stored"], 16 * 2 * TH)

        @block.gpsimd
        def _(pool):
            links = [0]

            def link(ins):
                links[0] += 1
                ins.then_inc(S["pool_link"], 1)
                pool.wait_ge(S["pool_link"], links[0])

            nc.gpsimd.memset(params_in, 0.0).then_inc(S["params_zero"], 1)
            link(nc.gpsimd.memset(ident[:], 0.0))
            nc.gpsimd.affine_select(out=ident[:], in_=ident[:], compare_op=ALU.not_equal, fill=1.0, base=0,
                                    pattern=[[-1, P]], channel_multiplier=1).then_inc(S["ident_ok"], 1)
            nc.gpsimd.memset(late[:, 0, 0:CT * P], 0.0).then_inc(S["matrices_zero"], 1)
            nc.gpsimd.memset(late[:, 1, 0:CT * P], 0.0).then_inc(S["matrices_zero"], 1)
            nc.gpsimd.iota(slot_iota[:], pattern=[[0, GROUPS], [1, SLOTS]], base=0, channel_multiplier=0,
                           allow_small_or_imprecise_dtypes=True)
            nc.gpsimd.iota(block_base[:], pattern=[[SLOTS, MAXB + 1]], base=0, channel_multiplier=0,
                           allow_small_or_imprecise_dtypes=True)
            nc.gpsimd.iota(part_iota[:], pattern=[[0, 1]], base=0, channel_multiplier=1,
                           allow_small_or_imprecise_dtypes=True)
            link(nc.gpsimd.memset(gated[:, 0, :], 1.0))
            link(nc.gpsimd.affine_select(out=gated[:, 1, :], in_=gated[:, 0, :], compare_op=ALU.is_gt, fill=0.0, base=0,
                                         pattern=[[1, P]], channel_multiplier=-1))
            nc.gpsimd.tensor_copy(before[:], gated[:, 1, :])
            nc.gpsimd.tensor_copy(ones_bf[:], gated[:, 0, :])
            pool.wait_ge(S["ident_ok"], 1)
            nc.gpsimd.tensor_scalar(scaled_ident, ident[:], alpha, None, ALU.mult)
            nc.gpsimd.memset(closed, 0.0).then_inc(S["closed_zero"], 1)
            nc.gpsimd.memset(small[:, 380:382], -0.5).then_inc(S["consts"], 1)
            nc.gpsimd.memset(back[:], 0.0).then_inc(S["back_sb"], 1)
            for h in range(TH):
                pool.wait_ge(S["var_ok"], h + 1)
                nc.gpsimd.tensor_tensor(small[:, 374 + h:375 + h], small[:, 370 + h:371 + h], small[:, 380:381], ALU.pow).then_inc(S["rstd_ok"], 1)
            pool.wait_ge(S["lpart_ps"], 1)
            nc.gpsimd.memset(y_sb[:, 0:512], 0.0).then_inc(S["y0_sb"], 1)
            nc.gpsimd.memset(y_sb[:, 512:D], 0.0).then_inc(S["y1_sb"], 1)
            for h in range(TH):
                pool.wait_ge(S["fin_var"], h + 1)
                nc.gpsimd.tensor_tensor(small[:, 374 + h:375 + h], small[:, 370 + h:371 + h], small[:, 380:381], ALU.pow).then_inc(S["fin_rstd"], 1)

        @block.scalar
        def _(act):
            for b in (0, 2):
                act.wait_ge(S["xt_ps"], b + 1)
                nc.scalar.copy(turned[:, 2 * b:2 * b + 2, :], ps[:, b, :].rearrange("p (k t) -> p k t", k=2)).then_inc(S["xt_act"], 1)
            act.wait_ge(S["matrices_zero"], 2)
            for dst, src in ((wr_bd, w_rgate), (wi_bd, w_igate)):
                heads = src[0].rearrange("(i two) r c -> two r i c", two=2)
                for s in range(2):
                    act.dma_start(dst[HD * s:HD * (s + 1), :, HD * s:HD * (s + 1)], heads[s]).then_inc(S["matrices_in"], 16)
            act.dma_start(wr[:], w_router[0].rearrange("(k p) e -> p k e", p=P)).then_inc(S["router_in"], 16)
            act.dma_start(b_rout[:], b_router[0:1, :].to_broadcast([P, E])).then_inc(S["router_in"], 16)

            act.wait_ge(S["lam_ok"], 1)
            nc.scalar.activation(small[:, 80:84], small[:, 76:80], ACT.Sigmoid).then_inc(S["lam_sig"], 1)
            act.wait_ge(S["proj"], 1)
            for b in range(2):
                nc.scalar.copy(rx[:, 2 * b:2 * b + 2, LW - 1:], ps[:, 4 + b, :].rearrange("p (i t) -> p i t", i=2)).then_inc(S["rx_sb"], 1)
            act.wait_ge(S["proj"], 2)
            for b in range(2):
                nc.scalar.copy(gel[:, 2 * b:2 * b + 2, :], ps[:, 6 + b, :].rearrange("p (i t) -> p i t", i=2)).then_inc(S["rg_sb"], 1)
            for n, (dst, off) in enumerate(((rgate, off_br), (igate, off_bi))):
                act.wait_ge(S["gates_ps"], n + 1)
                act.wait_ge(S["params_ok"], 1)
                for i in range(CT):
                    nc.scalar.activation(dst[:, i, :], half(4 + 2 * n + i // 2, i % 2), ACT.Sigmoid,
                                         bias=prm[:, off + i:off + i + 1]).then_inc(S["gate_sb"], 1)
            act.wait_ge(S["softplus_ok"], 1)
            act.wait_ge(S["gate_sb"], CT)
            for i in range(CT):
                nc.scalar.activation(rgate[:, i, :], rgate[:, i, :], ACT.Tanh, scale=small[:, 64 + i:65 + i]).then_inc(S["tanh_ok"], 1)
            act.wait_ge(S["gelu_in"], 1)
            nc.scalar.activation(gel2, gel2, ACT.Sigmoid, scale=GELU_IN).then_inc(S["gelu_sig"], 1)
            act.wait_ge(S["tanh_kept"], 1)
            nc.scalar.activation(rgate, rgate, ACT.Sqrt).then_inc(S["sqrt_ok"], 1)
            act.wait_ge(S["proj"], 3)
            for b in range(2):
                nc.scalar.copy(cv[:, 2 * b:2 * b + 2, CW - 1:], ps[:, b, :].rearrange("p (i t) -> p i t", i=2)).then_inc(S["cc_sb"], 1)
            for n in range(3):
                act.wait_ge(S["x1t_ps"], n + 1)
                nc.scalar.copy(x1t[:, n // 2, CT * (n % 2):CT * (n % 2 + 1), :],
                               ps[:, 4 + n, :].rearrange("p (k t) -> p k t", k=CT)).then_inc(S["x1t_act"], 1)
            act.wait_ge(S["lpart_ps"], 1)
            nc.scalar.copy(glu[:], half(HB, 0)).then_inc(S["lpart_sb"], 1)
            act.wait_ge(S["exp_in"], 1)
            nc.scalar.activation(small[:, 128:192], small[:, 64:128], ACT.Sigmoid).then_inc(S["exp_ok"], 1)
            act.wait_ge(S["rows0_ps"], 1)
            nc.scalar.copy(rows[:], half(Y0, 0)).then_inc(S["rows0_sb"], 1)
            act.wait_ge(S["rows0_t_ps"], 1)
            nc.scalar.copy(rows_t[:], half(Y0, 0).rearrange("p (b s) -> p b s", b=2)).then_inc(S["rows_t_ok"], 1)
            act.wait_ge(S["gates_t_ps"], 1)
            nc.scalar.copy(gates_t, ps[0:E, TB, 0:SEQ]).then_inc(S["gates_t_ok"], 1)

            act.wait_ge(S["bounds_ok"], 1)
            n_blocks = act.value_load(bounds[0:1, E:E + 1], min_val=1, max_val=MAXB)
            with act.Fori(0, n_blocks) as g:
                now = g + 1
                act.wait_ge(S["glu_ok"], now)
                nc.scalar.activation(sig[:], glu[:], ACT.Sigmoid, scale=SWIGLU_ALPHA).then_inc(S["sig_ok"], 1)
                act.wait_ge(S["rows_ps"], now)
                nc.scalar.copy(rows[:], half(Y0, 0)).then_inc(S["rows_sb"], 1)
                act.wait_ge(S["back_ps"], now)
                nc.scalar.copy(back[:], half(Y1, 0)).then_inc(S["back_sb"], 1)
                act.wait_ge(S["rows_t_ps"], now)
                nc.scalar.copy(rows_t[:], half(HB, 0).rearrange("p (b s) -> p b s", b=2)).then_inc(S["rows_t_ok"], 1)
                act.wait_ge(S["y0_ps"], now)
                nc.scalar.copy(y_sb[:, 0:512], ps[:, Y0, :]).then_inc(S["y0_sb"], 1)

        @block.vector
        def _(dve):
            V = nc.vector
            links = [0]

            def link(ins):
                links[0] += 1
                ins.then_inc(S["dve_link"], 1)
                dve.wait_ge(S["dve_link"], links[0])

            V.memset(rx[:, :, 0:LW - 1], 0.0)
            V.memset(cv[:, :, 0:CW - 1], 0.0)
            for b in (1, 3):
                dve.wait_ge(S["xt_ps"], b + 1)
                V.tensor_copy(turned[:, 2 * b:2 * b + 2, :], ps[:, b, :].rearrange("p (k t) -> p k t", k=2)).then_inc(S["xt_dve"], 1)
            dve.wait_ge(S["params_ps"], 1)
            V.tensor_copy(prm, ps[:, TB, 0:64]).then_inc(S["params_ok"], 1)
            dve.wait_ge(S["consts"], 1)
            V.tensor_reduce(stack_ident[:], ident[:].rearrange("p (j e) -> p e j", e=E), AX.X, ALU.add)
            lam = prm[:, off_lam:off_lam + CT]
            t = [small[:, 72 + CT * i:72 + CT * (i + 1)] for i in range(6)]
            dve.wait_ge(S["params_ok"], 1)
            link(V.tensor_scalar(t[0], lam, -1.0, None, ALU.mult))
            link(V.tensor_tensor(t[1], t[0], lam, ALU.min))
            V.tensor_scalar(t[5], t[0], 0.0, None, ALU.max).then_inc(S["lam_ok"], 1)
            dve.wait_ge(S["lam_sig"], 1)
            link(V.tensor_scalar(t[3], t[2], -1.0, 2.0, ALU.mult, ALU.add))
            link(V.reciprocal(t[4], t[3]))
            link(V.tensor_tensor(t[0], t[2], t[4], ALU.mult))
            link(V.tensor_tensor(t[1], t[0], t[0], ALU.mult))
            link(V.memset(t[3], 1.0 / 17))
            for n in range(7, -1, -1):
                link(V.tensor_tensor(t[4], t[3], t[1], ALU.mult))
                link(V.tensor_scalar(t[3], t[4], 1.0 / (2 * n + 1), None, ALU.add))
            link(V.scalar_tensor_tensor(t[2], t[0], 2.0, t[3], ALU.mult, ALU.mult))
            link(V.tensor_tensor(t[4], t[2], t[5], ALU.add))
            V.tensor_scalar(small[:, 64:64 + CT], t[4], LRU_C / 2, None, ALU.mult).then_inc(S["softplus_ok"], 1)
            for b in range(2):
                dve.wait_ge(S["rx_sb"], b + 1)
                for k in range(LW - 1, -1, -1):
                    for i in (2 * b, 2 * b + 1):
                        w = prm[:, off_lw + CT * k + i:off_lw + CT * k + i + 1]
                        if k == LW - 1:
                            ins = V.tensor_scalar(u[:, i, :], rx[:, i, k:k + SEQ], w, prm[:, off_lb + i:off_lb + i + 1], ALU.mult, ALU.add)
                        else:
                            ins = V.scalar_tensor_tensor(u[:, i, :], rx[:, i, k:k + SEQ], w, u[:, i, :], ALU.mult, ALU.add)
                    if k:
                        link(ins)
                ins.then_inc(S["u_ok"], 1)
            dve.wait_ge(S["rg_sb"], 2)
            dve.wait_ge(S["u_ok"], 2)
            link(V.tensor_tensor(gel2, gel, gel, ALU.mult))
            link(V.tensor_scalar(gel2, gel2, GELU_CUBE, 1.0, ALU.mult, ALU.add))
            V.tensor_tensor(gel2, gel2, gel, ALU.mult).then_inc(S["gelu_in"], 1)
            dve.wait_ge(S["tanh_ok"], CT)
            link(V.tensor_scalar(rec, rgate, 1.0, None, ALU.add))
            V.tensor_scalar(rgate, rgate, TINY, None, ALU.max).then_inc(S["tanh_kept"], 1)
            link(V.reciprocal(rec, rec))
            dve.wait_ge(S["gate_sb"], 2 * CT)
            link(V.tensor_tensor(igate, igate, u, ALU.mult))
            dve.wait_ge(S["sqrt_ok"], 1)
            link(V.scalar_tensor_tensor(rgate, rgate, 2.0, rec, ALU.mult, ALU.mult))
            link(V.tensor_tensor(igate, igate, rgate, ALU.mult))
            link(V.tensor_scalar(rec, rec, 2.0, -1.0, ALU.mult, ALU.add))
            for i in range(CT):
                ins = V.tensor_tensor_scan(u[:, i, :], rec[:, i, :], igate[:, i, :], 0.0, ALU.mult, ALU.add)
            link(ins)
            dve.wait_ge(S["gelu_sig"], 1)
            link(V.tensor_tensor(gel, gel, gel2, ALU.mult))
            V.tensor_tensor(mix[:, CT:KT, :], u, gel, ALU.mult).then_inc(S["mix_lru"], 1)
            dve.wait_ge(S["proj"], 4)
            dve.wait_ge(S["cc_sb"], 2)
            for b in range(2):
                V.tensor_tensor(cv[:, 2 * b:2 * b + 2, CW - 1:], cv[:, 2 * b:2 * b + 2, CW - 1:],
                                ps[:, 2 + b, :].rearrange("p (i t) -> p i t", i=2), ALU.mult).then_inc(S["ch_used"], 1)
            dve.wait_ge(S["ch_used"], 2)
            for k in range(CW):
                for i in range(CT):
                    w = prm[:, off_cw + CT * k + i:off_cw + CT * k + i + 1]
                    if k == 0:
                        ins = V.tensor_scalar(mix[:, i, :], cv[:, i, k:k + SEQ], w, None, ALU.mult)
                    else:
                        ins = V.scalar_tensor_tensor(mix[:, i, :], cv[:, i, k:k + SEQ], w, mix[:, i, :], ALU.mult, ALU.add)
                link(ins)
            dve.wait_ge(S["proj"], 5)
            for b in range(2):
                V.tensor_tensor(mix[:, 2 * b:2 * b + 2, :], mix[:, 2 * b:2 * b + 2, :],
                                ps[:, 4 + b, :].rearrange("p (i t) -> p i t", i=2), ALU.mult).then_inc(S["mix_conv"], 1)

            stats = small[:, 336:360].rearrange("p (h c s) -> p h c s", h=TH, c=2)
            mv = small[:, 360:364].rearrange("p (h s) -> p h s", h=TH)

            def norm_stats(h, c):
                return V.bn_stats(stats[:, h, c, :], ps[:, 2 * h + c, :])

            def norm_variance(h, var_sem):
                link(V.bn_aggr(mv[:, h, :], stats[:, h, :, :]))
                V.tensor_scalar(small[:, 370 + h:371 + h], mv[:, h, 1:2], LN_EPS, None, ALU.add).then_inc(var_sem, 1)

            def normalise(chunks, centred_sem, rstd_sem, done_sem):
                for n in range(len(chunks) + 1):
                    if n < len(chunks):
                        h, c = chunks[n]
                        v = ps[:, 2 * h + c, :]
                        V.scalar_tensor_tensor(v, v, mv[:, h, 0:1], late[:, 0, 512 * c:512 * c + 512], ALU.subtract, ALU.mult).then_inc(centred_sem, 1)
                    if n:
                        h, c = chunks[n - 1]
                        dve.wait_ge(centred_sem, 2 * h + c + 1)
                        dve.wait_ge(rstd_sem, h + 1)
                        V.scalar_tensor_tensor(xs[:, h, 512 * c:512 * c + 512], ps[:, 2 * h + c, :], small[:, 374 + h:375 + h],
                                               late[:, 1, 512 * c:512 * c + 512], ALU.mult, ALU.add).then_inc(done_sem, 1)

            dve.wait_ge(S["ln1_in"], 32)
            for h in range(TH):
                for c in range(2):
                    dve.wait_ge(S["out_ps"], 2 * h + c + 1)
                    v = ps[:, 2 * h + c, :]
                    link(V.scalar_tensor_tensor(v, xs[:, h, 512 * c:512 * c + 512], alpha, v, ALU.mult, ALU.add))
                    ins = norm_stats(h, c)
                link(ins)
                norm_variance(h, S["var_ok"])
                normalise([(h, 0), (h, 1)], S["centred"], S["rstd_ok"], S["x1_ok"])
            dve.wait_ge(S["x1t_ps"], 4)
            V.tensor_copy(x1t[:, 1, CT:KT, :], ps[:, 7, :].rearrange("p (k t) -> p k t", k=CT)).then_inc(S["x1t_dve"], 1)
            lg = small[:, 0:64].rearrange("p (h e) -> p h e", h=TH)
            shifted = small[:, 64:128].rearrange("p (h e) -> p h e", h=TH)
            sg = small[:, 128:192].rearrange("p (h e) -> p h e", h=TH)
            sel = small[:, 192:256].rearrange("p (h e) -> p h e", h=TH)
            ex = small[:, 256:320].rearrange("p (h e) -> p h e", h=TH)
            top = small[:, 320:336].rearrange("p (h k) -> p h k", h=TH)
            idx = small[:, 336:352].bitcast(U32).rearrange("p (h k) -> p h k", h=TH)
            idxf = small[:, 352:368].rearrange("p (h k) -> p h k", h=TH)
            total = small[:, 368:370]
            eye_row = slot_iota[:, 0, :]
            dve.wait_ge(S["logits_ps"], 1)
            dve.wait_ge(S["router_in"], 32)
            dve.wait_ge(S["x1_ok"], 2 * TH)
            link(V.tensor_tensor(lg, ps[:, Y0, 0:TH * E].rearrange("p (h e) -> p h e", h=TH),
                                 b_rout[:].unsqueeze(1).to_broadcast([P, TH, E]), ALU.add))
            for h in range(TH):
                ins = V.max(top[:, h, :], lg[:, h, :])
            link(ins)
            for h in range(TH):
                ins = V.max_index(idx[:, h, :], top[:, h, :], lg[:, h, :])
            ins.then_inc(S["dve_link"], 1)
            links[0] += 1
            V.tensor_tensor(shifted, lg, top[:, :, 0:1].to_broadcast([P, TH, E]), ALU.subtract).then_inc(S["exp_in"], 1)
            dve.wait_ge(S["dve_link"], links[0])
            link(V.tensor_copy(idxf, idx))
            hits = onehot[:].rearrange("p h j s -> p (h j s)").rearrange("p (h e k) -> p h e k", h=TH, k=TOP_K)
            link(V.tensor_tensor(hits, eye_row.unsqueeze(1).unsqueeze(3).to_broadcast([P, TH, E, TOP_K]),
                                 idxf[:, :, 0:TOP_K].unsqueeze(2).to_broadcast([P, TH, E, TOP_K]), ALU.is_equal))
            V.tensor_reduce(sel_bf, hits, AX.X, ALU.max).then_inc(S["sel_ok"], 1)
            link(V.tensor_reduce(sel, hits, AX.X, ALU.max))
            dve.wait_ge(S["rank_ps"], 1)
            rank = ps[:, TB, 0:TH * E].rearrange("p (h e) -> p h e", h=TH)
            link(V.scalar_tensor_tensor(places[:], rank, 1.0, sel, ALU.add, ALU.mult))
            for h in range(TH):
                ins = V.tensor_scalar(onehot[:, h], slot_iota[:], 1.0, places[:, h, 0:1], ALU.add, ALU.is_equal)
            ins.then_inc(S["onehot0"], 1)
            V.tensor_copy(bias_sel[:], ident_v[:, :, 0:1].to_broadcast([P, GROUPS, SLOTS])).then_inc(S["sel_bias"], 1)
            dve.wait_ge(S["exp_ok"], 1)
            nb_i = small[:, 64:96].bitcast(I32)
            nb_s = small[:, 96:128].bitcast(I32)
            nb, ends, zero = small[:, 320:352], small[:, 64:96], small[:, 0:32]
            cnt = ps[:, TB, 2 * E:3 * E]
            link(V.tensor_scalar(nb_i, cnt, 1.0, SLOTS - 1.0, ALU.max, ALU.add))
            V.memset(zero, 0.0)
            V.memset(bounds[:, 0:1], 0)
            link(V.tensor_scalar(nb_s, nb_i, SLOTS.bit_length() - 1, None, ALU.logical_shift_right))
            link(V.tensor_copy(nb, nb_s))
            link(V.tensor_tensor_scan(ends, nb, zero, 0.0, ALU.add, ALU.add))
            V.tensor_copy(bounds[0:1, 1:E + 1], ends[0:1, :]).then_inc(S["bounds_ok"], 1)
            link(V.tensor_scalar(small[:, 96:128], ends, part_iota[:], None, ALU.is_le))
            dve.wait_ge(S["closed_zero"], 1)
            V.tensor_reduce(closed[:, 0:1], small[:, 96:128], AX.X, ALU.add).then_inc(S["closed_ok"], 1)
            link(V.tensor_scalar(ex, sg, -1.0, 1.0, ALU.mult, ALU.add))
            link(V.reciprocal(ex, ex))
            link(V.tensor_tensor(ex, ex, sg, ALU.mult))
            link(V.tensor_tensor(ex, ex, sel, ALU.mult))
            link(V.tensor_reduce(total, ex, AX.X, ALU.add))
            link(V.reciprocal(total, total))
            V.tensor_tensor(gates[:], ex, total.unsqueeze(2).to_broadcast([P, TH, E]), ALU.mult).then_inc(S["gates_ok"], 1)
            dve.wait_ge(S["closed_ps"], 1)
            link(V.tensor_scalar(expert_of[:], ps[0:1, Y1, 0:P], E - 1.0, None, ALU.min))
            link(V.tensor_tensor(nb, ends, nb, ALU.subtract))
            link(V.scalar_tensor_tensor(sel, nb.unsqueeze(1).to_broadcast([P, TH, E]), float(SLOTS), sel, ALU.mult, ALU.mult))
            link(V.scalar_tensor_tensor(places[:], places[:], -1.0, sel, ALU.add, ALU.add))

            def pick(base, column):
                for h in range(TH):
                    ins = V.tensor_scalar(onehot[:, h], slot_iota[:], base, column(h), ALU.add, ALU.is_equal)
                return ins
            dve.wait_ge(S["rows0_ps"], 1)
            n_blocks = dve.value_load(bounds[0:1, E:E + 1], min_val=1, max_val=MAXB)
            with dve.Fori(0, n_blocks) as g:
                now = g + 1
                e = dve.value_load(expert_of[0:1, bass.ds(g, 1)], min_val=0, max_val=E - 1)
                e_next = dve.value_load(expert_of[0:1, bass.ds(now, 1)], min_val=0, max_val=E - 1)
                for h in range(TH):
                    ins = V.tensor_scalar(gated[:, h, :], onehot[:, h].rearrange("p j s -> p (j s)"), gates[:, h, bass.ds(e, 1)], None, ALU.mult)
                ins.then_inc(S["gated_ok"], 1)
                dve.wait_ge(S["gated_ok"], now)
                pick(block_base[:, bass.ds(now, 1)], lambda h: places[:, h, bass.ds(e_next, 1)]).then_inc(S["onehot_ok"], 1)
                dve.wait_ge(S["h_ps"], now)
                V.tensor_scalar(glu[:], half(HB, 0), SWIGLU_LIMIT, None, ALU.min).then_inc(S["glu_ok"], 1)
                V.tensor_scalar(lin[:], half(HB, 1), SWIGLU_LIMIT, -SWIGLU_LIMIT, ALU.min, ALU.max).then_inc(S["lin_ok"], 1)
                dve.wait_ge(S["lin_ok"], now)
                V.scalar_tensor_tensor(lin[:], lin[:], 1.0, glu[:], ALU.add, ALU.mult).then_inc(S["scaled_ok"], 1)
                dve.wait_ge(S["scaled_ok"], now)
                dve.wait_ge(S["sig_ok"], now)
                V.tensor_tensor(lin[:], lin[:], sig[:], ALU.mult).then_inc(S["act_ok"], 1)
                V.tensor_copy(bias_sel[:], ident_v[:, :, bass.ds(e_next, 1)].to_broadcast([P, GROUPS, SLOTS])).then_inc(S["sel_bias"], 1)
                dve.wait_ge(S["act_t_ps"], now)
                V.tensor_copy(act_t[:], half(TB, 0).rearrange("p (b s) -> p b s", b=2)).then_inc(S["act_t_sb"], 1)
                dve.wait_ge(S["y_ps"], now)
                V.tensor_copy(y_sb[:, 512:D], ps[:, Y1, :]).then_inc(S["y1_sb"], 1)
            dve.wait_ge(S["ln2_in"], 32)
            for c in range(2):
                for h in range(TH):
                    dve.wait_ge(S["acc_done"], TH * c + h + 1)
                    ins = norm_stats(h, c)
                    if c:
                        link(ins)
                        norm_variance(h, S["fin_var"])
            normalise([(h, c) for h in range(TH) for c in range(2)], S["fin_centred"], S["fin_rstd"], S["fin_ok"])

        @block.tensor
        def _(pe):
            T = nc.tensor
            pe.wait_ge(S["ident_ok"], 1)

            def keep_warm(bank, n):
                for _ in range(n):
                    T.matmul(ps[:, bank, 0:P], ident[:], ident[:], start=True, stop=True)
            keep_warm(TB, 5)
            for h in range(TH):
                pe.wait_ge(S[f"x_in{h}"], 16)
                for k in range(KT):
                    ins = T.transpose(ps[:, k // 2, 256 * (k % 2) + P * h:256 * (k % 2) + P * (h + 1)], xs[:, h, P * k:P * (k + 1)], ident[:])
                    if k % 2 and h == TH - 1:
                        ins.then_inc(S["xt_ps"], 1)

            def project(i, banks):
                pe.wait_ge(w_in_s[i], 16)
                for c in range(CT):
                    if i == RX and c == CT // 2:
                        pe.wait_ge(S["params_in"], 16 * 6)
                        T.transpose(ps[:, TB, 0:P], params_in, ident[:]).then_inc(S["params_ps"], 1)
                        pe.wait_ge(rx2_in, 16)
                    for k in range(KT):
                        ins = T.matmul(half(banks[c // 2], c % 2), w_piece[:, piece_slot[i], k, P * c:P * (c + 1)], turned[:, k, :],
                                       start=(k == 0), stop=(k == KT - 1))
                ins.then_inc(S["proj"], 1)
            keep_warm(TB, 7)
            pe.wait_ge(S["xt_act"], 2)
            pe.wait_ge(S["xt_dve"], 2)
            project(RX, (4, 5))
            pe.wait_ge(S["params_ok"], 1)
            project(RG, (6, 7))
            pe.wait_ge(S["u_ok"], 2)
            pe.wait_ge(S["matrices_in"], 64)
            pe.wait_ge(S["rx_sb"], 2)
            pe.wait_ge(S["rg_sb"], 2)
            for n, wt in enumerate((wr_bd, wi_bd)):
                for i in range(CT):
                    ins = T.matmul(half(4 + 2 * n + i // 2, i % 2), wt[:, i, :], u[:, i, :], start=True, stop=True)
                ins.then_inc(S["gates_ps"], 1)
            project(CC, (0, 1))
            project(CH, (2, 3))
            pe.wait_ge(S["gate_sb"], CT)
            project(CB, (4, 5))
            pe.wait_ge(S["mix_lru"], 1)
            pe.wait_ge(S["wout_in0"], 16)
            pe.wait_ge(S["cc_sb"], 2)
            pe.wait_ge(S["ch_used"], 2)

            def mixer_out(n, h, c, k):
                return T.matmul(ps[:, 2 * h + c, :], mix[:, k, P * h:P * (h + 1)], w_out_v[:, n, 512 * c:512 * c + 512],
                                start=(n == 0), stop=(n == KT - 1))
            for n in range(CT):
                for h in range(TH):
                    for c in range(2):
                        ins = mixer_out(n, h, c, CT + n)
            ins.then_inc(S["lru_out_ps"], 1)
            pe.wait_ge(S["mix_conv"], 2)
            pe.wait_ge(S["wout_in1"], 16)
            for h in range(TH):
                for c in range(2):
                    for n in range(CT):
                        ins = mixer_out(CT + n, h, c, n)
                    ins.then_inc(S["out_ps"], 1)

            def start_sum(h):
                for c in range(2):
                    T.matmul(ps[:, 2 * h + c, :], scaled_ident, xs[:, h, 512 * c:512 * c + 512],
                             start=True, stop=False, skip_group_check=True)
            pe.wait_ge(S["gate_sb"], 2 * CT)
            pe.wait_ge(S["router_in"], 32)
            per = KT // GROUPS
            for h in range(TH):
                for c in range(2):
                    if h and c == 0:
                        keep_warm(Y0, 5)
                    pe.wait_ge(S["x1_ok"], 2 * h + c + 1)
                    for k in range(CT):
                        ins = T.transpose(ps[:, 4 + 2 * h + c, P * k:P * (k + 1)], xs[:, h, P * (CT * c + k):P * (CT * c + k + 1)], ident[:])
                    ins.then_inc(S["x1t_ps"], 1)
                if h == 0:
                    start_sum(h)
                    pe.wait_ge(S["x1t_act"], 2)
                else:
                    keep_warm(Y0, 3)
                    pe.wait_ge(S["x1t_act"], 3)
                    pe.wait_ge(S["x1t_dve"], 1)
                for m in range(per):
                    for j in range(GROUPS):
                        ins = T.matmul(ps[SLOTS * j:SLOTS * (j + 1), HB, P * h:P * (h + 1)], wr[:, per * j + m, :], x1t[:, h, per * j + m, :],
                                       start=(m == 0), stop=(m == per - 1))
            ins.then_inc(S["lpart_ps"], 1)
            keep_warm(Y1, 1)
            pe.wait_ge(S["lpart_sb"], 1)
            for h in range(TH):
                ins = T.matmul(ps[:, Y0, E * h:E * (h + 1)], glu[:, P * h:P * (h + 1)], stack_ident[:], start=True, stop=True)
            ins.then_inc(S["logits_ps"], 1)
            start_sum(1)
            pe.wait_ge(S["sel_ok"], 1)
            T.matmul(ps[:, TB, 0:E], before[:], sel_bf[:, 0, :], start=True, stop=True)
            T.matmul(ps[:, TB, E:2 * E], ones_bf[:], sel_bf[:, 0, :], start=True, stop=False)
            T.matmul(ps[:, TB, E:2 * E], before[:], sel_bf[:, 1, :], start=False, stop=True)
            T.matmul(ps[:, TB, 2 * E:3 * E], ones_bf[:], sel_bf[:, 0, :], start=True, stop=False)
            T.matmul(ps[:, TB, 2 * E:3 * E], ones_bf[:], sel_bf[:, 1, :], start=False, stop=True).then_inc(S["rank_ps"], 1)

            def gather():
                for h in range(TH):
                    for j in range(GROUPS):
                        ins = T.matmul(ps[SLOTS * j:SLOTS * (j + 1), Y0, 0:QF], onehot[:, h, 0, :], xs[:, h, QF * j:QF * (j + 1)],
                                       start=(h == 0), stop=(h == TH - 1))
                return ins

            def turn(bank, src):
                for b in range(2):
                    ins = T.transpose(ps[:, bank, P * b:P * (b + 1)], src[:, P * b:P * (b + 1)], ident[:])
                return ins

            def combine(c):
                return [T.matmul(ps[:, 2 * h + c, :], back[:, P * h:P * (h + 1)], y_sb[:, 512 * c:512 * c + 512],
                                 start=False, stop=False, skip_group_check=True) for h in range(TH)]

            keep_warm(Y1, 4)
            pe.wait_ge(S["onehot0"], 1)
            gather().then_inc(S["rows0_ps"], 1)
            keep_warm(Y1, 2)
            pe.wait_ge(S["rows0_sb"], 1)
            for b in range(2):
                ins = T.transpose(ps[:, Y0, P * b:P * (b + 1)], rows[:, P * b:P * (b + 1)], ident[:])
            ins.then_inc(S["rows0_t_ps"], 1)
            pe.wait_ge(S["closed_ok"], 1)
            T.transpose(ps[:, Y1, 0:P], closed, ident[:]).then_inc(S["closed_ps"], 1)
            pe.wait_ge(S["bgu_in"], 16 * GROUPS)
            keep_warm(HB, 1)

            def turn_gates():
                pe.wait_ge(S["gates_ok"], 1)
                for h in range(TH):
                    ins = T.transpose(ps[0:E, TB, P * h:P * (h + 1)], gates[:, h, :], ident[:])
                ins.then_inc(S["gates_t_ps"], 1)

            def expert_block(now, after, b, loads, down, first=False):
                pe.wait_ge(S["rows_t_ok"], now)
                for c in range(GC):
                    pe.wait_ge(gu_in[b][c], loads)
                    for k in range(GK * c, GK * (c + 1)):
                        for j in range(GROUPS):
                            ins = T.matmul(ps[SLOTS * j:SLOTS * (j + 1), HB, :],
                                           rows_t[:, k % 2, SLOTS * (k // 2):SLOTS * (k // 2 + 1)],
                                           gu_buf[:, b, k, :].rearrange("p (two n) -> p two n", two=2)[:, :, QF * j:QF * (j + 1)],
                                           start=(k == 0), stop=False)
                    if c < GC - 1:
                        ins.then_inc(gu_used[c], 1)
                    if first and c == 1:
                        turn_gates()
                pe.wait_ge(S["sel_bias"], now)
                for j in range(GROUPS):
                    ins = T.matmul(ps[SLOTS * j:SLOTS * (j + 1), HB, :], bias_sel[:, j, :], b_gu, start=False, stop=True)
                ins.then_inc(S["h_ps"], 1)
                pe.wait_ge(S["onehot_ok"], now)
                pe.wait_ge(S["y0_sb"], now)
                gather().then_inc(S["rows_ps"], 1)
                pe.wait_ge(S["back_sb"], now)
                combine(0)
                pe.wait_ge(S["act_ok"], now)
                turn(TB, lin).then_inc(S["act_t_ps"], 1)
                pe.wait_ge(S["y1_sb"], now)
                combine(1)
                pe.wait_ge(S["gated_ok"], now)
                turn(Y1, gated[:].rearrange("p h n -> p (h n)")).then_inc(S["back_ps"], 1)
                pe.wait_ge(S["rows_sb"], now)
                turn(HB, rows).then_inc(S["rows_t_ps"], 1)
                pe.wait_ge(S["act_t_sb"], now)
                for m in range(DC):
                    landed, count, weights = down[m]
                    pe.wait_ge(landed, count)
                    for c in range(2):
                        if m == 0 and c == 1:
                            pe.wait_ge(S["back_sb"], after)
                        for j in range(GROUPS):
                            ins = T.matmul(ps[SLOTS * j:SLOTS * (j + 1), Y0 + c, :], act_t[:, m, SLOTS * j:SLOTS * (j + 1)],
                                           weights[j][:, 512 * c:512 * c + 512], start=(m == 0), stop=(m == DC - 1))
                        if m == DC - 1 and c == 0:
                            ins.then_inc(S["y0_ps"], 1)
                    if m == 0:
                        ins.then_inc(dn_used[0], 1)
                ins.then_inc(S["y_ps"], 1)

            def down_at(m, count):
                return dn_in[m], count, [dn_buf[:, m, j, :] for j in range(GROUPS)]

            def expert(e, b, loads, down):
                first = pe.value_load(bounds[0:1, bass.ds(e, 1)], min_val=1, max_val=MAXB - 1)
                end = pe.value_load(bounds[0:1, bass.ds(e + 1, 1)], min_val=1, max_val=MAXB)
                with pe.Fori(first, end) as g:
                    expert_block(g + 1, g + 2, b, loads, down)

            down_0 = [down_at(m, 16) for m in range(DC)]
            expert_block(1, 2, 0, 16, down_0, first=True)
            pe.wait_ge(S["bounds_ok"], 1)
            end = pe.value_load(bounds[0:1, 1:2], min_val=1, max_val=MAXB)
            with pe.If(end > 1):
                with pe.Fori(1, end) as g:
                    expert_block(g + 1, g + 2, 0, 16, down_0)
            expert(1, 1, 16, [(S["extra_in"], 16 * GROUPS, dn_extra), down_at(1, 32)])

            def pair_of_experts(pair):
                for b in range(2):
                    e = pair * 2 + b
                    expert(e, b, (pair + 1) * 16, [down_at(0, e * 16), down_at(1, (e + 1) * 16)])

            with pe.Fori(1, E // 2 - 1) as pair:
                pair_of_experts(pair)
            pe.wait_ge(S["bdn_in"], 16)
            pe.wait_ge(S["gates_t_ok"], 1)
            for h in range(TH):
                for c in range(2):
                    T.matmul(ps[:, 2 * h + c, :], gates_t[:, P * h:P * (h + 1)], b_dn[:, 512 * c:512 * c + 512],
                             start=False, stop=False, skip_group_check=True)
            with pe.Fori(E // 2 - 1, E // 2) as pair:
                pair_of_experts(pair)
            n_blocks = pe.value_load(bounds[0:1, E:E + 1], min_val=1, max_val=MAXB)
            pe.wait_ge(S["y0_sb"], n_blocks + 1)
            pe.wait_ge(S["back_sb"], n_blocks + 1)
            for c in range(2):
                if c:
                    pe.wait_ge(S["y1_sb"], n_blocks + 1)
                for ins in combine(c):
                    ins.then_inc(S["acc_done"], 1)


_INS = ["x", "w_in", "conv_w", "lru_conv_w", "lru_conv_b", "w_rgate", "b_rgate", "w_igate", "b_igate", "lru_lambda", "w_out",
        "ln1_g", "ln1_b", "w_router", "b_router", "w_gate_up", "b_gate_up", "w_down", "b_down", "ln2_g", "ln2_b"]


def kernel(**inputs):
    import numpy as _np
    import concourse.bacc as _bacc
    from concourse.bass_utils import run_bass_kernel_spmd as _run

    nc = _bacc.Bacc("TRN2", target_bir_lowering=False, num_devices=1)
    arrays, args = {}, []
    for name in _INS:
        a = _np.ascontiguousarray(inputs[name])
        arrays[f"in_{name}_dram"] = a
        args.append(nc.dram_tensor(f"in_{name}_dram", a.shape, mybir.dt.from_np(a.dtype), kind="ExternalInput").ap())
    shape = _np.shape(inputs["x"])
    args.append(nc.dram_tensor("out_0_dram", shape, F32, kind="ExternalOutput").ap())
    trunk(nc, *args)
    r = _run(nc, [arrays], core_ids=[0])
    return r.results[0]["out_0_dram"]
```
